# Optimizing a Trainium2 kernel written in Bass

```python
import jax, jax.numpy as jnp
from jax import lax
import numpy as np

D_MODEL = 1024
BATCH = 1
SEQ = 512
DEPTH = 1
DEC_BATCH = 8
DEC_SEQ = 1
PAST_LEN = 4096
PAGE_SIZE = 128

D_CONV = D_MODEL
D_POOL = D_MODEL // 2
N_POOL_GROUPS = 4
POOL_GROUP = D_POOL // N_POOL_GROUPS
POOL_OUT_GROUP = D_MODEL // N_POOL_GROUPS
POOL_WINDOWS = (2, 4, 8, 16)
POOL_STATE = max(POOL_WINDOWS) - 1
CONV_WIDTH = 3
D_FF = ((8 * D_MODEL // 3 + 127) // 128) * 128
ALPHA = (2.0 * DEPTH) ** 0.25
BETA = (8.0 * DEPTH) ** -0.25
LN_EPS = 1e-5
SPLITS = [D_CONV, 2 * D_CONV, 3 * D_CONV, 3 * D_CONV + D_POOL, 3 * D_CONV + D_POOL + D_MODEL]
D_IN = 3 * D_CONV + D_POOL + 2 * D_MODEL

kernel_name = "gated_conv_pool_macaron_deepnorm_step"

def layer_norm(x, g, b):
    xf = x.astype(jnp.float32)
    mu = jnp.mean(xf, axis=-1, keepdims=True)
    var = jnp.mean(jnp.square(xf - mu), axis=-1, keepdims=True)
    y = (xf - mu) * lax.rsqrt(var + LN_EPS)
    return (y * g.astype(jnp.float32) + b.astype(jnp.float32)).astype(x.dtype)

def swiglu(x, wg, wu, wd):
    hid = jax.nn.silu(jnp.einsum('btd,df->btf', x, wg)) * jnp.einsum('btd,df->btf', x, wu)
    return jnp.einsum('btf,fd->btd', hid, wd)

def short_conv(u_ext, conv_w, t_new):
    out = conv_w[0] * u_ext[:, 0:t_new]
    for k in range(1, CONV_WIDTH):
        out = out + conv_w[k] * u_ext[:, k:k + t_new]
    return out

def multiscale_pool(p_ext, pos0, t_new):
    pf = p_ext.astype(jnp.float32)
    bsz = pf.shape[0]
    cs = jnp.concatenate([jnp.zeros((bsz, 1, D_POOL), jnp.float32), jnp.cumsum(pf, axis=1)], axis=1)
    pos = pos0 + jnp.arange(t_new)
    outs = []
    for g, w in enumerate(POOL_WINDOWS):
        sl = slice(g * POOL_GROUP, (g + 1) * POOL_GROUP)
        hi = cs[:, POOL_STATE + 1:POOL_STATE + 1 + t_new, sl]
        lo = cs[:, POOL_STATE + 1 - w:POOL_STATE + 1 - w + t_new, sl]
        cnt = jnp.minimum(pos + 1, w).astype(jnp.float32)[None, :, None]
        outs.append((hi - lo) / cnt)
    mean = jnp.concatenate(outs, axis=-1)
    return (mean - pf[:, POOL_STATE:]).astype(p_ext.dtype)

def hybrid_layer(x, conv_state, pool_state, pos0, ln1_g, ln1_b, ffn1_wg, ffn1_wu, ffn1_wd,
                 w_in, conv_w, pool_w, pool_scale, w_out, ln2_g, ln2_b,
                 ffn2_wg, ffn2_wu, ffn2_wd, ln3_g, ln3_b):
    bsz, t_new, _ = x.shape
    x = layer_norm(ALPHA * x + 0.5 * swiglu(x, ffn1_wg, ffn1_wu, ffn1_wd), ln1_g, ln1_b)
    z = jnp.einsum('btd,de->bte', x, w_in)
    c_g, b_g, h, p, g_a, g_p = jnp.split(z, SPLITS, axis=-1)
    u = c_g * h
    u_ext = jnp.concatenate([conv_state.astype(u.dtype), u], axis=1)
    y_a = b_g * short_conv(u_ext, conv_w, t_new)
    p_ext = jnp.concatenate([pool_state.astype(p.dtype), p], axis=1)
    q = multiscale_pool(p_ext, pos0, t_new)
    y_p = jnp.einsum('btgc,gce->btge', q.reshape(bsz, t_new, N_POOL_GROUPS, POOL_GROUP), pool_w)
    y_p = y_p.reshape(bsz, t_new, D_MODEL) * pool_scale
    m = jax.nn.sigmoid(g_a) * y_a + jax.nn.sigmoid(g_p) * y_p
    x = layer_norm(ALPHA * x + jnp.einsum('btd,de->bte', m, w_out), ln2_g, ln2_b)
    x = layer_norm(ALPHA * x + 0.5 * swiglu(x, ffn2_wg, ffn2_wu, ffn2_wd), ln3_g, ln3_b)
    return x, u_ext[:, -(CONV_WIDTH - 1):], p_ext[:, -POOL_STATE:]

def setup_inputs(seed: int = 0) -> dict:
    key = jax.random.key(seed)
    ks = jax.random.split(key, 24)
    f32 = jnp.float32
    nrm = lambda k, shape, s: jax.random.normal(k, shape, f32) * s
    L = DEPTH
    return {
        "x_prompt": nrm(ks[0], (BATCH, SEQ, D_MODEL), 1.0),
        "x_sample": nrm(ks[1], (DEC_BATCH, DEC_SEQ, D_MODEL), 1.0),
        "state_conv": nrm(ks[2], (L, DEC_BATCH, CONV_WIDTH - 1, D_CONV), 1.0),
        "state_pool": nrm(ks[3], (L, DEC_BATCH, POOL_STATE, D_POOL), 1.0),
        "ln1_g": 1.0 + nrm(ks[4], (L, D_MODEL), 0.02),
        "ln1_b": nrm(ks[5], (L, D_MODEL), 0.02),
        "ffn1_wg": nrm(ks[6], (L, D_MODEL, D_FF), D_MODEL ** -0.5),
        "ffn1_wu": nrm(ks[7], (L, D_MODEL, D_FF), D_MODEL ** -0.5),
        "ffn1_wd": nrm(ks[8], (L, D_FF, D_MODEL), BETA * D_FF ** -0.5),
        "w_in": nrm(ks[9], (L, D_MODEL, D_IN), D_MODEL ** -0.5),
        "conv_w": nrm(ks[10], (L, CONV_WIDTH, D_CONV), CONV_WIDTH ** -0.5),
        "pool_w": nrm(ks[11], (L, N_POOL_GROUPS, POOL_GROUP, POOL_OUT_GROUP), POOL_GROUP ** -0.5),
        "pool_scale": 1.0 + nrm(ks[12], (L, D_MODEL), 0.02),
        "w_out": nrm(ks[13], (L, D_MODEL, D_MODEL), BETA * D_MODEL ** -0.5),
        "ln2_g": 1.0 + nrm(ks[14], (L, D_MODEL), 0.02),
        "ln2_b": nrm(ks[15], (L, D_MODEL), 0.02),
        "ffn2_wg": nrm(ks[16], (L, D_MODEL, D_FF), D_MODEL ** -0.5),
        "ffn2_wu": nrm(ks[17], (L, D_MODEL, D_FF), D_MODEL ** -0.5),
        "ffn2_wd": nrm(ks[18], (L, D_FF, D_MODEL), BETA * D_FF ** -0.5),
        "ln3_g": 1.0 + nrm(ks[19], (L, D_MODEL), 0.02),
        "ln3_b": nrm(ks[20], (L, D_MODEL), 0.02),
    }

def reference(x_prompt, x_sample, state_conv, state_pool, ln1_g, ln1_b, ffn1_wg, ffn1_wu, ffn1_wd,
              w_in, conv_w, pool_w, pool_scale, w_out, ln2_g, ln2_b,
              ffn2_wg, ffn2_wu, ffn2_wd, ln3_g, ln3_b):
    bp = x_prompt.shape[0]
    yp, ys = x_prompt, x_sample
    conv_p, pool_p, conv_s, pool_s = [], [], [], []
    for l in range(DEPTH):
        w = (ln1_g[l], ln1_b[l], ffn1_wg[l], ffn1_wu[l], ffn1_wd[l], w_in[l], conv_w[l], pool_w[l],
             pool_scale[l], w_out[l], ln2_g[l], ln2_b[l], ffn2_wg[l], ffn2_wu[l], ffn2_wd[l],
             ln3_g[l], ln3_b[l])
        zc = jnp.zeros((bp, CONV_WIDTH - 1, D_CONV), yp.dtype)
        zp = jnp.zeros((bp, POOL_STATE, D_POOL), yp.dtype)
        yp, cp, pp = hybrid_layer(yp, zc, zp, 0, *w)
        ys, cs_, ps_ = hybrid_layer(ys, state_conv[l], state_pool[l], PAST_LEN, *w)
        conv_p.append(cp); pool_p.append(pp); conv_s.append(cs_); pool_s.append(ps_)
    return (yp, ys, jnp.stack(conv_p), jnp.stack(pool_p), jnp.stack(conv_s), jnp.stack(pool_s))


_drawn_inputs = setup_inputs


def setup_inputs(seed=0):
    import zlib

    import numpy as np

    out = dict(_drawn_inputs(seed))
    spreads = {}
    factors = {'pool_scale': 8.0, 'ln2_g': 2.842, 'ln2_b': 2.844, 'ln3_g': 2.834, 'ln3_b': 2.948}
    for name, (base, spread) in spreads.items():
        noise = np.random.default_rng([zlib.crc32(name.encode()), seed]).standard_normal(out[name].shape)
        drawn = base * np.exp(spread * noise) if base else spread * noise
        out[name] = __import__('jax').numpy.asarray(drawn.astype(out[name].dtype))
    for name, factor in factors.items():
        out[name] = (out[name] * factor).astype(out[name].dtype)
    return out
```

```python
from contextlib import ExitStack

import concourse.bass as bass
from concourse import mybir

ALU = mybir.AluOpType
ACT = mybir.ActivationFunctionType
AX_X = mybir.AxisListType.X
F32 = mybir.dt.float32
F32R = mybir.dt.float32r

P = 128
LN_EPS = 1e-5
POOL_WINDOWS = (2, 4, 8, 16)
RAW = 2
SLOTS = 6
BLOCKS = 8


class Signal:

    def __init__(self, sem):
        self.sem, self.n = sem, 0

    def on(self, ins):
        ins.then_inc(self.sem, 1)
        self.n += 1
        return self.n


def build(nc, x_prompt, x_sample, state_conv, state_pool, ln1_g, ln1_b, ffn1_wg, ffn1_wu, ffn1_wd,
          w_in, conv_w, pool_w, pool_scale, w_out, ln2_g, ln2_b, ffn2_wg, ffn2_wu, ffn2_wd,
          ln3_g, ln3_b, y_prompt, y_sample, conv_prompt, pool_prompt, conv_sample, pool_sample):
    depth, D, FF = ffn1_wg.shape
    T = x_prompt.shape[1]
    NS = x_sample.shape[0] * x_sample.shape[1]
    PS = state_pool.shape[2]
    CS = state_conv.shape[2]
    assert depth == 1 and x_prompt.shape[0] == 1 and x_sample.shape[1] == 1
    ALPHA = (2.0 * depth) ** 0.25
    N = T + NS
    H = N // 2
    HB = T - H
    K = D // P
    KF = FF // P
    G = len(POOL_WINDOWS)
    TT = T // P
    assert K == BLOCKS and KF == 22 and K == 2 * G and N % 4 == 0 and H <= 512
    DQ = [(0, 8), (8, 8), (16, KF - 16)]
    NSHIFT = K - 2

    UP = [0, 124]
    DOWN = [UP[0] + 2 * KF, UP[1] + 2 * KF]
    MIX = DOWN[0] + 3 * K
    OUT = MIX + 12 * G
    assert OUT + K == UP[1]
    CHUNKS = DOWN[1] + 3 * K
    assert CHUNKS % SLOTS == 0

    with ExitStack() as ctx:
        def sb(name, shape, dt=F32):
            return ctx.enter_context(nc.sbuf_tensor(name, shape, dt))

        def sem(name):
            return ctx.enter_context(nc.semaphore(name))

        x32 = sb("x32", [P, K, N])
        xh = sb("xh", [P, K, N], F32R)
        xl = sb("xl", [P, K, N], F32R)
        raw = sb("raw", [P, RAW, BLOCKS, P])
        wh = sb("wh", [P, SLOTS, BLOCKS, P], F32R)
        wl = sb("wl", [P, SLOTS, BLOCKS, P], F32R)
        par = sb("par", [P, 10 * K])
        ident = sb("ident", [P, P])
        ones_shift = sb("ones_shift", [P, P])
        ones_mean = sb("ones_mean", [P, P])
        conv_state = sb("conv_state", [P, K, NS, CS])
        pool_state = sb("pool_state", [P, G, NS, PS])
        scratch = sb("scratch", [P, 3 * N + 3 * H])
        gate = scratch[:, 0:2 * N].rearrange("p (s n) -> p s n", s=2)
        hid32 = scratch[:, 2 * N:3 * N]
        tile_sum = scratch[:, 0:N]
        square_sum = scratch[:, N:2 * N]
        square = scratch[:, 2 * N:3 * N]
        offset = scratch[:, 3 * N:3 * N + H]
        variance = scratch[:, 3 * N + H:3 * N + 2 * H]
        rstd = scratch[:, 3 * N + 2 * H:3 * N + 3 * H]

        def phase(*tensors):
            with ExitStack() as over:
                return [over.enter_context(nc.sbuf_tensor(name, shape, dt)) for name, shape, dt in tensors]

        xrow, srow, prow, csrow, psrow = phase(
            ("xrow", [P, TT, D], F32), ("srow", [NS, D], F32), ("prow", [10 * K, P], F32),
            ("csrow", [NS * CS, D], F32), ("psrow", [NS * PS, G * P], F32))
        hid = [None, None]
        hid[0] = phase(("hid1_hi", [P, KF, N], F32R), ("hid1_lo", [P, KF, N], F32R))
        WP = 16 + T
        (mh, ml, pext, psmp, win, q32, qh, ql, csb, uext, usmp, ymix, vmix, sga, sgp, yp, rcount, first,
         sampsum, utail, ptail, utrow, ptrow) = phase(
            ("mh", [P, K, N], F32R), ("ml", [P, K, N], F32R), ("pext", [P, WP], F32),
            ("psmp", [P, NS, 16], F32), ("win", [P, 2, WP], F32), ("q32", [P, N], F32),
            ("qh", [P, N], F32R), ("ql", [P, N], F32R), ("csb", [P, N], F32), ("uext", [P, 2 + T], F32),
            ("usmp", [P, NS, 3], F32), ("ymix", [P, N], F32), ("vmix", [P, N], F32), ("sga", [P, N], F32),
            ("sgp", [P, N], F32), ("yp", [P, 2, N], F32), ("rcount", [P, 16], F32), ("first", [P, 16], F32),
            ("sampsum", [P, NS], F32), ("utail", [P, K, CS + NS], F32), ("ptail", [P, G, PS + NS], F32),
            ("utrow", [CS + NS, D], F32), ("ptrow", [PS + NS, G * P], F32))
        hid[1] = phase(("hid2_hi", [P, KF, N], F32R), ("hid2_lo", [P, KF, N], F32R))
        yrow, ysrow = phase(("yrow", [P, TT, D], F32), ("ysrow", [NS, D], F32))

        ps = ctx.enter_context(nc.psum_tensor("ps", [P, 8, 512], F32))

        def bank(pair, h):
            return ps[:, 2 * pair + h, 0:H]

        def pair_of(pair):
            return ps[:, 2 * pair:2 * pair + 2, 0:H]

        def two(ap):
            return ap.rearrange("p (h n) -> p h n", h=2)

        def half(ap, h):
            return ap[:, h * H:(h + 1) * H]

        rows_in = sem("rows_in")
        small_in = sem("small_in")
        const_ready = sem("const_ready")
        cols_made = sem("cols_made")
        cols_read = sem("cols_read")
        x_round = sem("x_round")
        x_ready = sem("x_ready")
        raw_in = [sem(f"raw_in{r}") for r in range(RAW)]
        hi_ready = sem("hi_ready")
        lo_ready = sem("lo_ready")
        w_used = sem("w_used")
        out_done = sem("out_done")

        class Ffn:
            def __init__(self, n):
                self.gate_on = sem(f"gate_on{n}")
                self.gated = sem(f"gated{n}")
                self.hid_made = sem(f"hid_made{n}")
                self.hid_round = sem(f"hid_round{n}")
                self.hid_ready = sem(f"hid_ready{n}")

        class Norm:
            def __init__(self, n):
                self.turn = sem(f"turn{n}")
                self.summed = sem(f"summed{n}")
                self.shift = sem(f"shift{n}")
                self.tail_shifted = sem(f"tail_shifted{n}")
                self.half_done = sem(f"half_done{n}")
                self.centred = sem(f"centred{n}")
                self.squared = sem(f"squared{n}")
                self.c_sum = sem(f"c_sum{n}")
                self.q_sum = sem(f"q_sum{n}")
                self.stats = sem(f"stats{n}")
                self.chain = sem(f"chain{n}")
                self.rooted = sem(f"rooted{n}")
                self.minus = sem(f"minus{n}")
                self.scaled = sem(f"scaled{n}")
                self.affine = sem(f"affine{n}")
                self.ready = sem(f"ready{n}")

        ffn = [Ffn(1), Ffn(2)]
        norm = [Norm(1), Norm(2), Norm(3)]

        p_link = sem("p_link")
        q_made = sem("q_made")
        q_round = sem("q_round")
        q_ready = sem("q_ready")
        c_copied = sem("c_copied")
        u_made = sem("u_made")
        ya_made = sem("ya_made")
        sga_made = sem("sga_made")
        sgp_made = sem("sgp_made")
        yp_copied = sem("yp_copied")
        a_gated = sem("a_gated")
        p_gated = sem("p_gated")
        m_made = sem("m_made")
        m_round = sem("m_round")
        m_ready = sem("m_ready")
        tails_turned = sem("tails_turned")
        tails_copied = sem("tails_copied")
        tails_out = sem("tails_out")
        y_turned = sem("y_turned")
        y_copied = [sem("y_copied_act"), sem("y_copied_dve")]

        def blocks(w):
            return w[0].rearrange("(k p) n -> p k n", p=P)

        wg_v, wu_v, wd_v = ([blocks(a), blocks(b)] for a, b in (
            (ffn1_wg, ffn2_wg), (ffn1_wu, ffn2_wu), (ffn1_wd, ffn2_wd)))
        win_v, wout_v = blocks(w_in), blocks(w_out)
        C_AT, B_AT, H_AT, P_AT = 0, K, 2 * K, 3 * K
        GA_AT, GP_AT = P_AT + G, P_AT + G + K

        UP_LOOP = (KF - 4) // 6

        def up_tiles(eng, body):
            for f in (0, 1):
                body(f, f)
            with eng.Fori(0, UP_LOOP) as i:
                for j in range(6):
                    body(i * 6 + (2 + j), 2 + j)
            for f in (KF - 2, KF - 1):
                body(f, f)

        block = ctx.enter_context(nc.Block())

        @block.sync
        def _(sp):
            def load(c, place, src, wait=True):
                n = src.shape[1]
                if wait:
                    sp.wait_ge(lo_ready, c - (RAW - 1))
                sp.dma_start(raw[:, place % RAW, 0:n, :], src).then_inc(raw_in[place % RAW], 16)

            for t in range(TT):
                sp.dma_start(xrow[:, t, :], x_prompt[0, t * P:(t + 1) * P, :]).then_inc(rows_in, 16)

            def column(v, f):
                return v[:, :, bass.ds(f * P, P)]

            for n in range(2):
                def up(f, place):
                    c, cs = 2 * f + UP[n], 2 * place + UP[n]
                    first_chunks = n == 0 and isinstance(f, int) and f == 0
                    load(c, cs, column(wg_v[n], f), not first_chunks)
                    load(c + 1, cs + 1, column(wu_v[n], f), not first_chunks)
                up_tiles(sp, up)
                with sp.Fori(0, K // 2) as i:
                    for j in range(2):
                        for q, (k0, nk) in enumerate(DQ):
                            c = i * 6 + (DOWN[n] + 3 * j + q)
                            load(c, DOWN[n] + 3 * j + q, wd_v[n][:, k0:k0 + nk, bass.ds(i * (2 * P) + j * P, P)])
                if n == 1:
                    break
                with sp.Fori(0, G) as g:
                    def mix(place, v):
                        load(g * 12 + (MIX + place), MIX + place, v)
                    mix(0, column(win_v, g + P_AT))
                    for j in range(2):
                        at = 1 if j == 0 else 7
                        mix(at, column(win_v, g * 2 + (C_AT + j)))
                        mix(at + 1, column(win_v, g * 2 + (H_AT + j)))
                        mix(at + 2, column(win_v, g * 2 + (B_AT + j)))
                        if j == 0:
                            mix(4, pool_w[0, bass.ds(g, 1), :, :].rearrange("g p (j n) -> p (g j) n", n=P))
                            at = 2
                        mix(at + 3, column(win_v, g * 2 + (GA_AT + j)))
                        mix(at + 4, column(win_v, g * 2 + (GP_AT + j)))
                for d in range(K):
                    load(OUT + d, OUT + d, column(wout_v, d))

            for t in range(TT):
                sp.wait_ge(y_copied[0], t + 1)
                sp.wait_ge(y_copied[1], t + 1)
                sp.dma_start(y_prompt[0, t * P:(t + 1) * P, :], yrow[:, t, :]).then_inc(out_done, 16)
            sp.wait_ge(y_copied[0], TT + 1)
            sp.wait_ge(y_copied[1], TT + 1)
            sp.dma_start(y_sample.rearrange("b t d -> (b t) d"), ysrow[:]).then_inc(out_done, 16)
            sp.wait_ge(out_done, 16 * (TT + 1 + 2))
            sp.wait_ge(tails_out, 16 * 4)

        @block.gpsimd
        def _(pool):
            made = Signal(const_ready)
            made.on(nc.gpsimd.memset(ident[:], 0.0))
            pool.wait_ge(const_ready, 1)
            made.on(nc.gpsimd.affine_select(out=ident[:], in_=ident[:], compare_op=ALU.not_equal, fill=1.0,
                                            base=0, pattern=[[-1, P]], channel_multiplier=1))
            made.on(nc.gpsimd.memset(ones_shift[:], 1.0 / (NSHIFT * P)))
            made.on(nc.gpsimd.memset(ones_mean[:], 1.0 / D))
            assert made.n == 4
            with pool.Fori(0, CHUNKS // SLOTS) as i:
                for j in range(SLOTS):
                    pool.wait_ge(hi_ready, i * SLOTS + (j + 1))
                    nc.gpsimd.tensor_tensor(wl[:, j], raw[:, j % RAW], wh[:, j].bitcast(F32),
                                            ALU.subtract).then_inc(lo_ready, 1)

        @block.scalar
        def _(act):
            def copy(out, in_):
                return nc.scalar.activation(out, in_, ACT.Copy)

            def round_chunk(c, place, free=True):
                if isinstance(c, int) and c >= CHUNKS:
                    return
                if free:
                    act.wait_ge(w_used, c - (SLOTS - 1))
                if isinstance(c, int):
                    act.wait_ge(raw_in[place % RAW], 16 * (c // RAW + 1))
                else:
                    act.wait_ge(raw_in[place % RAW], c * 8 + (16 - 8 * (place % RAW)))
                copy(wh[:, place % SLOTS], raw[:, place % RAW]).then_inc(hi_ready, 1)

            act.dma_start(srow[:], x_sample.rearrange("b t d -> (b t) d")).then_inc(small_in, 16)
            for n, v in enumerate((ln1_g, ln1_b, ln2_g, ln2_b, ln3_g, ln3_b, pool_scale)):
                act.dma_start(prow[n * K:(n + 1) * K, :], v[0].rearrange("(k p) -> k p", p=P)).then_inc(small_in, 16)
            act.dma_start(prow[7 * K:10 * K, :], conv_w[0].rearrange("w (k p) -> (w k) p", p=P)).then_inc(small_in, 16)
            act.dma_start(csrow[:], state_conv[0].rearrange("b s d -> (b s) d")).then_inc(small_in, 16)
            act.dma_start(psrow[:], state_pool[0].rearrange("b s d -> (b s) d")).then_inc(small_in, 16)
            act.dma_start(conv_sample[0, :, 0:CS - 1, :], state_conv[0, :, 1:CS, :]).then_inc(out_done, 16)
            act.dma_start(pool_sample[0, :, 0:PS - 1, :], state_pool[0, :, 1:PS, :]).then_inc(out_done, 16)

            round_chunk(0, 0, False)
            round_chunk(1, 1, False)
            for k in range(K):
                act.wait_ge(cols_read, 5 + k)
                copy(xh[:, k, :], x32[:, k, :]).then_inc(x_round, 1)
                if k % 2 == 1:
                    round_chunk(2 + k // 2, 2 + k // 2, False)

            def ffn_steps(n):
                s = ffn[n]

                def up(f, place):
                    c, cs = 2 * f + UP[n], 2 * place + UP[n]
                    pair = 2 * (place % 2)
                    act.wait_ge(w_used, c + 1)
                    if not (isinstance(f, int) and f < 2):
                        act.wait_ge(s.gated, f - 1)
                    nc.scalar.activation(two(gate[:, place % 2, :]), pair_of(pair),
                                         ACT.Sigmoid).then_inc(s.gate_on, 1)
                    round_chunk(c + SLOTS, cs + SLOTS)
                    round_chunk(c + 1 + SLOTS, cs + 1 + SLOTS)
                    act.wait_ge(s.hid_made, f + 1)
                    if n == 1 and isinstance(f, int) and f == 0:
                        act.wait_ge(tails_out, 64)
                    copy(hid[n][0][:, bass.ds(f, 1), :].rearrange("p a n -> p (a n)"), hid32).then_inc(s.hid_round, 1)
                up_tiles(act, up)
                with act.Fori(0, 3) as i:
                    for j in range(6):
                        round_chunk(i * 6 + (DOWN[n] + j + SLOTS), DOWN[n] + j + SLOTS)

            def norm_steps(n, g_at, b_at, next_chunks, last=False):
                s = norm[n]
                for t in range(NSHIFT):
                    act.wait_ge(s.centred, t + 1)
                    if t >= 1:
                        act.wait_ge(s.q_sum, t)
                    nc.scalar.activation(square, x32[:, t, :], ACT.Square).then_inc(s.squared, 1)
                rounds = list(next_chunks)

                def tile_half(m, t, h):
                    act.wait_ge(s.centred, m + 1)
                    act.wait_ge(s.q_sum, m)
                    nc.scalar.activation(half(square, h), half(x32[:, t, :], h), ACT.Square).then_inc(s.squared, 1)

                def normalise(h):
                    act.wait_ge(s.chain, 9 * h + 4)
                    nc.scalar.activation(rstd, variance, ACT.Sqrt).then_inc(s.rooted, 1)
                    if h == 0:
                        tile_half(NSHIFT + 2, NSHIFT, 1)
                    for kk in range(K // 2):
                        act.wait_ge(s.scaled, 4 * h + kk + 1)
                        for k in (2 * kk, 2 * kk + 1):
                            v = half(x32[:, k, :], h)
                            if not last:
                                nc.scalar.activation(half(xh[:, k, :], h), v, ACT.Identity,
                                                     bias=par[:, b_at + k:b_at + k + 1],
                                                     scale=par[:, g_at + k:g_at + k + 1])
                            ins = nc.scalar.activation(v, v, ACT.Identity, bias=par[:, b_at + k:b_at + k + 1],
                                                       scale=par[:, g_at + k:g_at + k + 1])
                        ins.then_inc(s.affine, 1)
                        if rounds:
                            c = rounds.pop(0)
                            round_chunk(c, c)

                tile_half(NSHIFT, NSHIFT, 0)
                tile_half(NSHIFT + 1, NSHIFT + 1, 0)
                normalise(0)
                tile_half(NSHIFT + 3, NSHIFT + 1, 1)
                normalise(1)
                for c in rounds:
                    round_chunk(c, c)

            ffn_steps(0)
            norm_steps(0, 0, K, range(MIX, MIX + SLOTS))

            def reused(used, times):
                if not (isinstance(times, int) and times == 0):
                    act.wait_ge(used, times)

            def mix_group(g):
                def next_chunk(j):
                    round_chunk(g * 12 + (MIX + j + SLOTS), MIX + j + SLOTS)

                def copy_c(j, at):
                    act.wait_ge(w_used, g * 12 + (MIX + at + 1))
                    reused(u_made, g * 2 + j)
                    copy(two(csb[:]), pair_of(1 if j == 0 else 0)).then_inc(c_copied, 1)

                def gates(j, at):
                    act.wait_ge(w_used, g * 12 + (MIX + at + 1))
                    reused(a_gated, g * 2 + j)
                    nc.scalar.activation(two(sga[:]), pair_of(2 if j == 0 else 3), ACT.Sigmoid).then_inc(sga_made, 1)
                    next_chunk(at)
                    act.wait_ge(w_used, g * 12 + (MIX + at + 2))
                    reused(p_gated, g * 2 + j)
                    nc.scalar.activation(two(sgp[:]), pair_of(3 if j == 0 else 1), ACT.Sigmoid).then_inc(sgp_made, 1)
                    next_chunk(at + 1)
                    act.wait_ge(m_made, g * 2 + (j + 1))
                    copy(mh[:, bass.ds(g * 2 + j, 1), :].rearrange("p a n -> p (a n)"), ymix[:]).then_inc(m_round, 1)

                next_chunk(0)
                copy_c(0, 1)
                next_chunk(1)
                act.wait_ge(q_made, g + 1)
                copy(qh[:], q32[:]).then_inc(q_round, 1)
                next_chunk(2)
                next_chunk(3)
                act.wait_ge(w_used, g * 12 + (MIX + 5))
                reused(p_gated, g * 2)
                for j in range(2):
                    copy(two(yp[:, j, :]), pair_of(j)).then_inc(yp_copied, 1)
                next_chunk(4)
                gates(0, 5)
                copy_c(1, 7)
                next_chunk(7)
                next_chunk(8)
                next_chunk(9)
                gates(1, 10)

            mix_group(0)
            with act.Fori(1, G) as g:
                mix_group(g)

            round_chunk(UP[1] - 2 + 0, UP[1] - 2)
            round_chunk(UP[1] - 1, UP[1] - 1)
            act.wait_ge(tails_turned, 1)
            copied = Signal(tails_copied)
            for b in range(2):
                copied.on(copy(utrow[:, b * 512:(b + 1) * 512], ps[0:CS + NS, 6 + b, :]))
            copied.on(copy(ptrow[:], ps[0:PS + NS, 4, :]))
            act.wait_ge(tails_copied, 3)
            act.dma_start(conv_prompt[0, 0], utrow[0:CS, :]).then_inc(tails_out, 16)
            act.dma_start(conv_sample[0, :, CS - 1, :], utrow[CS:CS + NS, :]).then_inc(tails_out, 16)
            act.dma_start(pool_prompt[0, 0], ptrow[0:PS, :]).then_inc(tails_out, 16)
            act.dma_start(pool_sample[0, :, PS - 1, :], ptrow[PS:PS + NS, :]).then_inc(tails_out, 16)
            for c in range(UP[1], UP[1] + 4):
                round_chunk(c, c)
            norm_steps(1, 2 * K, 3 * K, range(UP[1] + 4, UP[1] + SLOTS))
            ffn_steps(1)
            norm_steps(2, 4 * K, 5 * K, (), last=True)
            for t in range(TT + 1):
                act.wait_ge(y_turned, t + 1)
                if t < TT:
                    copy(yrow[:, t, 0:512], ps[:, 2 * t, :]).then_inc(y_copied[0], 1)
                else:
                    copy(ysrow[:, 0:512], ps[0:NS, 0, :]).then_inc(y_copied[0], 1)

        @block.vector
        def _(dve):
            tt, ts, stt = nc.vector.tensor_tensor, nc.vector.tensor_scalar, nc.vector.scalar_tensor_tensor
            copy = nc.vector.tensor_copy

            read = Signal(cols_read)
            dve.wait_ge(cols_made, 1)
            read.on(copy(x32[:, :, T:N], ps[:, 7, 0:K * NS].rearrange("p (k n) -> p k n", k=K)))
            read.on(copy(par[:], ps[:, 7, 128:128 + 10 * K]))
            read.on(copy(conv_state[:].rearrange("p k b s -> p (k b s)"), ps[:, 7, 208:208 + K * NS * CS]))
            dve.wait_ge(cols_made, 2)
            read.on(copy(pool_state[:].rearrange("p g b s -> p (g b s)"), ps[:, 6, 0:G * NS * PS]))

            def x_lo(k):
                dve.wait_ge(x_round, k + 1)
                tt(xl[:, k, :], x32[:, k, :], xh[:, k, :].bitcast(F32), ALU.subtract).then_inc(x_ready, 1)
            for k in range(K):
                dve.wait_ge(cols_made, 3 + k)
                read.on(copy(x32[:, k, 0:T], ps[:, k, :]))
                if k >= 1:
                    x_lo(k - 1)
            x_lo(K - 1)

            def up_steps(n):
                s = ffn[n]

                def up(f, place):
                    pair = 2 * (place % 2)
                    g = gate[:, place % 2, :]
                    dve.wait_ge(s.gate_on, f + 1)
                    tt(two(g), two(g), pair_of(pair), ALU.mult).then_inc(s.gated, 1)
                    dve.wait_ge(s.gated, f + 1)
                    dve.wait_ge(w_used, 2 * f + (UP[n] + 2))
                    tt(two(hid32), two(g), pair_of(pair + 1), ALU.mult).then_inc(s.hid_made, 1)
                    dve.wait_ge(s.hid_made, f + 1)
                    dve.wait_ge(s.hid_round, f + 1)
                    one = bass.ds(f, 1)
                    tt(hid[n][1][:, one, :].rearrange("p a n -> p (a n)"), hid32,
                       hid[n][0][:, one, :].rearrange("p a n -> p (a n)").bitcast(F32),
                       ALU.subtract).then_inc(s.hid_ready, 1)
                up_tiles(dve, up)

            def norm_steps(n, start, per, weight, last=False):
                s = norm[n]
                ts(x32[:], x32[:], ALPHA, None, ALU.mult).then_inc(s.turn, 1)
                nc.vector.memset(tile_sum, 0.0).then_inc(s.turn, 1)
                dve.wait_ge(s.turn, 2)
                for t in range(NSHIFT):
                    dve.wait_ge(w_used, start + per * (t + 1))
                    y = two(x32[:, t, :])
                    stt(y, pair_of(t % 2), weight, y, ALU.mult, ALU.add).then_inc(s.turn, 1)
                    dve.wait_ge(s.turn, t + 3)
                    if t:
                        dve.wait_ge(s.summed, t)
                    tt(tile_sum, tile_sum, x32[:, t, :], ALU.add).then_inc(s.summed, 1)
                dve.wait_ge(s.shift, 2)
                shift = pair_of(2)
                for t in (NSHIFT, NSHIFT + 1):
                    y = two(x32[:, t, :])
                    tt(y, y, shift, ALU.subtract).then_inc(s.tail_shifted, 1)
                for t in range(NSHIFT):
                    y = two(x32[:, t, :])
                    tt(y, y, shift, ALU.subtract).then_inc(s.centred, 1)

                def add(m, c, h=None):
                    part = (lambda a: a) if h is None else (lambda a: half(a, h))
                    dve.wait_ge(s.centred, m + 1)
                    if m == 0:
                        copy(tile_sum, c).then_inc(s.c_sum, 1)
                        dve.wait_ge(s.squared, 1)
                        copy(square_sum, square).then_inc(s.q_sum, 1)
                        return
                    dve.wait_ge(s.c_sum, m)
                    tt(part(tile_sum), part(tile_sum), c, ALU.add).then_inc(s.c_sum, 1)
                    dve.wait_ge(s.squared, m + 1)
                    dve.wait_ge(s.q_sum, m)
                    tt(part(square_sum), part(square_sum), part(square), ALU.add).then_inc(s.q_sum, 1)

                for t in range(NSHIFT):
                    add(t, x32[:, t, :])

                def tile_half(m, t, h):
                    if h == 0:
                        dve.wait_ge(s.half_done, t - NSHIFT + 1)
                    else:
                        dve.wait_ge(w_used, start + per * (t + 1))
                    dve.wait_ge(s.tail_shifted, 2)
                    y = half(x32[:, t, :], h)
                    stt(y, bank(t % 2, h), weight, y, ALU.mult, ALU.add).then_inc(s.centred, 1)
                    add(m, y, h)

                def normalise(h):
                    link = Signal(s.chain)
                    link.n = 9 * h

                    def then(ins):
                        dve.wait_ge(s.chain, link.on(ins))
                    var, t = variance, half(square, h)
                    dve.wait_ge(s.stats, h + 1)
                    then(copy(offset, bank(3, h)))
                    then(tt(var, offset, bank(3, h), ALU.mult))
                    then(tt(var, bank(2, h), var, ALU.subtract))
                    then(ts(var, var, 0.0, LN_EPS, ALU.max, ALU.add))
                    dve.wait_ge(s.rooted, h + 1)
                    then(nc.vector.reciprocal(rstd, rstd))
                    then(tt(t, rstd, rstd, ALU.mult))
                    then(tt(t, t, var, ALU.mult))
                    then(ts(t, t, -0.5, 1.5, ALU.mult, ALU.add))
                    then(tt(rstd, rstd, t, ALU.mult))
                    assert link.n == 9 * (h + 1)
                    if h == 0:
                        tile_half(NSHIFT + 2, NSHIFT, 1)

                    def lo(kk):
                        dve.wait_ge(s.affine, 4 * h + kk + 1)
                        v = slice(2 * kk, 2 * kk + 2), slice(h * H, (h + 1) * H)
                        tt(xl[:, v[0], v[1]], x32[:, v[0], v[1]], xh[:, v[0], v[1]].bitcast(F32),
                           ALU.subtract).then_inc(s.ready, 1)
                    for kk in range(K // 2):
                        v = x32[:, 2 * kk:2 * kk + 2, h * H:(h + 1) * H]
                        tt(v, v, offset.unsqueeze(1).broadcast_to([P, 2, H]), ALU.subtract).then_inc(s.minus, 1)
                        dve.wait_ge(s.minus, 4 * h + kk + 1)
                        tt(v, v, rstd.unsqueeze(1).broadcast_to([P, 2, H]), ALU.mult).then_inc(s.scaled, 1)
                        if kk >= 1 and not last:
                            lo(kk - 1)
                    if not last:
                        lo(K // 2 - 1)

                tile_half(NSHIFT, NSHIFT, 0)
                tile_half(NSHIFT + 1, NSHIFT + 1, 0)
                normalise(0)
                tile_half(NSHIFT + 3, NSHIFT + 1, 1)
                normalise(1)

            up_steps(0)
            norm_steps(0, DOWN[0], 3, 0.5)

            link = Signal(p_link)

            def then(ins):
                dve.wait_ge(p_link, link.on(ins))

            then(nc.vector.memset(pext[:, 0:16], 0.0))
            then(nc.vector.memset(uext[:, 0:2], 0.0))
            for i in range(15):
                then(nc.vector.memset(rcount[:, i:i + 1], 1.0 / (i + 1)))
            for g, w in enumerate(POOL_WINDOWS):
                base = MIX + 12 * g
                dve.wait_ge(w_used, base + 1)
                link.on(copy(psmp[:, :, 0:PS], pool_state[:, g]))
                link.on(copy(pext[:, 16:16 + H], bank(0, 0)))
                link.on(copy(psmp[:, :, PS], bank(0, 1)[:, HB:H]))
                then(copy(pext[:, 16 + H:16 + T], bank(0, 1)[:, 0:HB]))
                link.on(copy(ptail[:, g, 0:PS], pext[:, 16 + T - PS:16 + T]))
                link.on(copy(ptail[:, g, PS:PS + NS], psmp[:, :, PS]))
                src = pext[:]
                level = 0
                while (1 << level) < w:
                    s, lo = 1 << level, 2 * (1 << level) - 1
                    dst = win[:, level % 2, :]
                    then(tt(dst[:, lo:WP], src[:, lo:WP], src[:, lo - s:WP - s], ALU.add))
                    src, level = dst, level + 1
                then(nc.vector.tensor_reduce(sampsum[:], psmp[:, :, PS + 1 - w:PS + 1], AX_X, ALU.add))
                then(tt(first[:, 0:w - 1], src[:, 16:16 + w - 1], rcount[:, 0:w - 1], ALU.mult))
                link.on(stt(q32[:, w - 1:T], src[:, 16 + w - 1:WP], 1.0 / w, pext[:, 16 + w - 1:WP],
                            ALU.mult, ALU.subtract))
                link.on(stt(q32[:, T:N], sampsum[:], 1.0 / w, psmp[:, :, PS], ALU.mult, ALU.subtract))
                dve.wait_ge(p_link, link.n)
                tt(q32[:, 0:w - 1], first[:, 0:w - 1], pext[:, 16:16 + w - 1], ALU.subtract).then_inc(q_made, 1)
                dve.wait_ge(q_made, g + 1)
                dve.wait_ge(q_round, g + 1)
                tt(ql[:], q32[:], qh[:].bitcast(F32), ALU.subtract).then_inc(q_ready, 1)
                for j in range(2):
                    t = 2 * g + j
                    at = base + (1 if j == 0 else 7)
                    c_pair, h_pair, b_pair = ((1, 2, 3), (0, 1, 2))[j]
                    dve.wait_ge(w_used, at + 2)
                    dve.wait_ge(c_copied, t + 1)
                    link.on(copy(usmp[:, :, 0:CS], conv_state[:, t]))
                    link.on(tt(uext[:, 2:2 + H], csb[:, 0:H], bank(h_pair, 0), ALU.mult))
                    then(tt(usmp[:, :, CS], csb[:, T:N], bank(h_pair, 1)[:, HB:H], ALU.mult))
                    tt(uext[:, 2 + H:2 + T], csb[:, H:T], bank(h_pair, 1)[:, 0:HB], ALU.mult).then_inc(u_made, 1)
                    dve.wait_ge(u_made, t + 1)
                    link.on(copy(utail[:, t, 0:CS], uext[:, T:T + 2]))
                    link.on(copy(utail[:, t, CS:CS + NS], usmp[:, :, CS]))
                    for i in range(3):
                        wi = par[:, 7 * K + i * K + t:7 * K + i * K + t + 1]
                        parts = ((ymix[:, 0:T], uext[:, i:i + T]), (ymix[:, T:N], usmp[:, :, i]))
                        for y, u in parts:
                            if i == 0:
                                link.on(ts(y, u, wi, None, ALU.mult))
                            else:
                                link.on(stt(y, u, wi, y, ALU.mult, ALU.add))
                        dve.wait_ge(p_link, link.n)
                    dve.wait_ge(w_used, at + 3)
                    tt(two(ymix[:]), two(ymix[:]), pair_of(b_pair), ALU.mult).then_inc(ya_made, 1)
                    dve.wait_ge(ya_made, t + 1)
                    dve.wait_ge(sga_made, t + 1)
                    tt(ymix[:], ymix[:], sga[:], ALU.mult).then_inc(a_gated, 1)
                    dve.wait_ge(yp_copied, t + 1)
                    dve.wait_ge(sgp_made, t + 1)
                    stt(vmix[:], yp[:, j, :], par[:, 6 * K + t:6 * K + t + 1], sgp[:],
                        ALU.mult, ALU.mult).then_inc(p_gated, 1)
                    dve.wait_ge(a_gated, t + 1)
                    dve.wait_ge(p_gated, t + 1)
                    tt(ymix[:], ymix[:], vmix[:], ALU.add).then_inc(m_made, 1)
                    dve.wait_ge(m_made, t + 1)
                    dve.wait_ge(m_round, t + 1)
                    tt(ml[:, t, :], ymix[:], mh[:, t, :].bitcast(F32), ALU.subtract).then_inc(m_ready, 1)

            norm_steps(1, OUT, 1, 1.0)
            dve.wait_ge(tails_out, 64)
            up_steps(1)
            norm_steps(2, DOWN[1], 3, 0.5, last=True)
            for t in range(TT + 1):
                dve.wait_ge(y_turned, t + 1)
                if t < TT:
                    copy(yrow[:, t, 512:1024], ps[:, 2 * t + 1, :]).then_inc(y_copied[1], 1)
                else:
                    copy(ysrow[:, 512:1024], ps[0:NS, 1, :]).then_inc(y_copied[1], 1)

        @block.tensor
        def _(pe):
            mm = nc.tensor.matmul

            def run(out, blocks_, start=True, stop=True):
                todo = [b for b in blocks_ if not callable(b)]
                n = 0
                for b in blocks_:
                    if callable(b):
                        b()
                        continue
                    slot, k, vh, vl = b
                    n += 1
                    mm(out, wh[:, slot, k, :], vh, start=start and n == 1, stop=False)
                    mm(out, wh[:, slot, k, :], vl, start=False, stop=False)
                    ins = mm(out, wl[:, slot, k, :], vh, start=False, stop=stop and n == len(todo))
                return ins

            def x_blocks(slot, h, ready=None):
                out = []
                for k in range(K):
                    if ready is not None:
                        out.append(lambda k=k: ready(h, k))
                    out.append((slot, k, half(xh[:, k, :], h), half(xl[:, k, :], h)))
                return out

            def product(c, place, pair):
                pe.wait_ge(lo_ready, c + 1)
                for h in range(2):
                    ins = run(bank(pair, h), x_blocks(place % SLOTS, h))
                ins.then_inc(w_used, 1)

            def opening(c, ready, between=None):
                for h in range(2):
                    for j in range(4):
                        if h == 0:
                            pe.wait_ge(lo_ready, c + j + 1)
                        ins = run(bank(j, h), x_blocks((c + j) % SLOTS, h, ready if j == 0 else None))
                        if h == 1:
                            ins.then_inc(w_used, 1)
                        if h == 0 and j == 0 and between is not None:
                            between()

            def input_ready(h, k):
                pe.wait_ge(x_ready, k + 1)

            def norm_ready(n):
                def ready(h, k):
                    if k % 2 == 0:
                        pe.wait_ge(norm[n].ready, 4 * h + k // 2 + 1)
                return ready

            def shift_sums(n):
                s = norm[n]
                pe.wait_ge(s.summed, NSHIFT)
                for h in range(2):
                    mm(bank(2, h), ones_shift[:], half(tile_sum, h), start=True, stop=True).then_inc(s.shift, 1)

            def stat_sums(n, h):
                s = norm[n]
                m = NSHIFT + 2 * (h + 1)
                pe.wait_ge(s.c_sum, m)
                pe.wait_ge(s.q_sum, m)
                mm(bank(3, h), ones_mean[:], half(tile_sum, h), start=True, stop=True)
                mm(bank(2, h), ones_mean[:], half(square_sum, h), start=True, stop=True).then_inc(s.stats, 1)

            def closing(n, c, chunks_of, vectors, ready=None):
                s = norm[n]
                for h in range(2):
                    for t in range(2):
                        if h == 0:
                            pe.wait_ge(s.turn, NSHIFT + t + 1)
                        for q in range(chunks_of):
                            ch = c + chunks_of * t + q
                            if h == 0:
                                pe.wait_ge(lo_ready, ch + 1)
                            ins = run(bank(t, h), vectors(ch, q, h), start=q == 0, stop=q == chunks_of - 1)
                            if h == 1:
                                ins.then_inc(w_used, 1)
                            elif q == chunks_of - 1:
                                ins.then_inc(s.half_done, 1)
                            if h == 0 and t == 0 and q == 0:
                                shift_sums(n)
                            if h == 1 and t == 0 and q == 0:
                                stat_sums(n, 0)

            def hid_blocks(n, slot, q, h, wait=False):
                k0, nk = DQ[q]
                out = []
                for k in range(nk):
                    if wait:
                        out.append(lambda k=k: pe.wait_ge(ffn[n].hid_ready, k0 + k + 1))
                    out.append((slot, k, half(hid[n][0][:, k0 + k, :], h), half(hid[n][1][:, k0 + k, :], h)))
                return out

            def ffn_steps(n, ready, between=None):
                s = ffn[n]

                def up(f, place):
                    if isinstance(f, int) and f < 2:
                        return
                    pair = 2 * (place % 2)
                    pe.wait_ge(s.gated, f - 1)
                    product(2 * f + UP[n], 2 * place + UP[n], pair)
                    pe.wait_ge(s.hid_made, f - 1)
                    product(2 * f + (UP[n] + 1), 2 * place + UP[n] + 1, pair + 1)
                opening(UP[n], ready, between)
                up_tiles(pe, up)
                pe.wait_ge(s.hid_made, KF - 1)
                with pe.Fori(0, 3) as i:
                    for j in range(2):
                        pe.wait_ge(norm[2 * n].turn, i * 2 + (j + 1))
                        for h in range(2):
                            for q in range(3):
                                place = DOWN[n] + 3 * j + q
                                if h == 0:
                                    pe.wait_ge(lo_ready, i * 6 + (place + 1))
                                ins = run(bank(j, h), hid_blocks(n, place % SLOTS, q, h, j == 0 and h == 0),
                                          start=q == 0, stop=q == 2)
                                if h == 1:
                                    ins.then_inc(w_used, 1)
                pe.wait_ge(s.hid_made, KF)
                closing(2 * n, DOWN[n] + 18, 3, lambda ch, q, h: hid_blocks(n, ch % SLOTS, q, h))

            pe.wait_ge(const_ready, 4)
            pe.wait_ge(small_in, 16 * 11)
            for k in range(K):
                nc.tensor.transpose(ps[:, 7, k * NS:(k + 1) * NS], srow[:, k * P:(k + 1) * P], ident[0:NS, 0:NS])
                cw = NS * CS
                nc.tensor.transpose(ps[:, 7, 208 + k * cw:208 + (k + 1) * cw], csrow[:, k * P:(k + 1) * P],
                                    ident[0:cw, 0:cw])
            nc.tensor.transpose(ps[:, 7, 128:128 + 10 * K], prow[:], ident[0:10 * K, 0:10 * K]).then_inc(cols_made, 1)
            for g in range(G):
                pw = NS * PS
                ins = nc.tensor.transpose(ps[:, 6, g * pw:(g + 1) * pw], psrow[:, g * P:(g + 1) * P], ident[0:pw, 0:pw])
            ins.then_inc(cols_made, 1)
            pe.wait_ge(rows_in, 16 * TT)
            for k in range(K):
                if k == 6:
                    pe.wait_ge(cols_read, 4)
                for t in range(TT):
                    ins = nc.tensor.transpose(ps[:, k, t * P:(t + 1) * P], xrow[:, t, k * P:(k + 1) * P], ident[:])
                ins.then_inc(cols_made, 1)

            ffn_steps(0, input_ready)

            def mix_group(g, opened):
                def wproduct(at, pair):
                    product(g * 12 + (MIX + at), MIX + at, pair)

                if not opened:
                    pe.wait_ge(yp_copied, g * 2 - 1)
                    wproduct(0, 0)
                    pe.wait_ge(sgp_made, g * 2)
                    wproduct(1, 1)
                    pe.wait_ge(ya_made, g * 2)
                    wproduct(2, 2)
                    pe.wait_ge(sga_made, g * 2)
                    wproduct(3, 3)
                pe.wait_ge(lo_ready, g * 12 + (MIX + 5))
                pe.wait_ge(q_ready, g + 1)
                pe.wait_ge(c_copied, g * 2 + 1)
                slot = (MIX + 4) % SLOTS
                for j in range(2):
                    for h in range(2):
                        ins = run(bank(j, h), [(slot, j, half(qh[:], h), half(ql[:], h))])
                ins.then_inc(w_used, 1)
                pe.wait_ge(u_made, g * 2 + 1)
                wproduct(5, 2)
                pe.wait_ge(ya_made, g * 2 + 1)
                wproduct(6, 3)
                pe.wait_ge(yp_copied, g * 2 + 1)
                wproduct(7, 0)
                pe.wait_ge(yp_copied, g * 2 + 2)
                wproduct(8, 1)
                pe.wait_ge(sga_made, g * 2 + 1)
                wproduct(9, 2)
                pe.wait_ge(sgp_made, g * 2 + 1)
                wproduct(10, 3)
                pe.wait_ge(u_made, g * 2 + 2)
                wproduct(11, 1)

            opening(MIX, norm_ready(0), lambda: stat_sums(0, 1))
            mix_group(0, True)
            with pe.Fori(1, G) as g:
                mix_group(g, False)

            def m_blocks(slot, h, wait=False):
                out = []
                for k in range(K):
                    if wait:
                        out.append(lambda k=k: pe.wait_ge(m_ready, k + 1))
                    out.append((slot, k, half(mh[:, k, :], h), half(ml[:, k, :], h)))
                return out

            pe.wait_ge(c_copied, K)
            for d in range(NSHIFT):
                if d == 1:
                    pe.wait_ge(sgp_made, K)
                pe.wait_ge(norm[1].turn, d + 1)
                pe.wait_ge(lo_ready, OUT + d + 1)
                for h in range(2):
                    ins = run(bank(d % 2, h), m_blocks((OUT + d) % SLOTS, h, d == 0 and h == 0))
                ins.then_inc(w_used, 1)
                if d == 1:
                    for g in range(G):
                        nc.tensor.transpose(ps[0:PS + NS, 4, g * P:(g + 1) * P], ptail[:, g, :], ident[:])
                    for t in range(K):
                        ins = nc.tensor.transpose(ps[0:CS + NS, 6 + t // 4, (t % 4) * P:(t % 4 + 1) * P],
                                                  utail[:, t, :], ident[:])
                    ins.then_inc(tails_turned, 1)
            pe.wait_ge(tails_copied, 3)
            closing(1, OUT + NSHIFT, 1, lambda ch, q, h: m_blocks(ch % SLOTS, h))

            ffn_steps(1, norm_ready(1), lambda: stat_sums(1, 1))
            stat_sums(2, 1)

            for t in range(TT):
                pe.wait_ge(norm[2].affine, 4 if (t + 1) * P <= H else 8)
                for k in range(K):
                    ins = nc.tensor.transpose(ps[:, 2 * t + k // 4, (k % 4) * P:(k % 4 + 1) * P],
                                              x32[:, k, t * P:(t + 1) * P], ident[:])
                ins.then_inc(y_turned, 1)
            pe.wait_ge(y_copied[0], 1)
            pe.wait_ge(y_copied[1], 1)
            for k in range(K):
                ins = nc.tensor.transpose(ps[0:NS, k // 4, (k % 4) * P:(k % 4 + 1) * P], x32[:, k, T:N], ident[:])
            ins.then_inc(y_turned, 1)


_INS = ["x_prompt", "x_sample", "state_conv", "state_pool", "ln1_g", "ln1_b", "ffn1_wg", "ffn1_wu", "ffn1_wd",
        "w_in", "conv_w", "pool_w", "pool_scale", "w_out", "ln2_g", "ln2_b", "ffn2_wg", "ffn2_wu", "ffn2_wd",
        "ln3_g", "ln3_b"]


def kernel(**inputs):
    import numpy as _np
    import concourse.bacc as _bacc
    from concourse import mybir as _mybir
    from concourse.bass_utils import run_bass_kernel_spmd as _run

    nc = _bacc.Bacc("TRN2", target_bir_lowering=False, num_devices=1)
    arrays, args = {}, []
    for name in _INS:
        a = _np.ascontiguousarray(inputs[name])
        arrays[f"in_{name}_dram"] = a
        args.append(nc.dram_tensor(f"in_{name}_dram", a.shape, _mybir.dt.from_np(a.dtype), kind="ExternalInput").ap())
    depth, batch, cs, d = inputs["state_conv"].shape
    _, _, ps, dp = inputs["state_pool"].shape
    pb = inputs["x_prompt"].shape[0]
    outs = [inputs["x_prompt"].shape, inputs["x_sample"].shape, (depth, pb, cs, d), (depth, pb, ps, dp),
            (depth, batch, cs, d), (depth, batch, ps, dp)]
    for i, shape in enumerate(outs):
        args.append(nc.dram_tensor(f"out_{i}_dram", shape, F32, kind="ExternalOutput").ap())
    build(nc, *args)
    r = _run(nc, [arrays], core_ids=[0])
    return tuple(r.results[0][f"out_{i}_dram"] for i in range(len(outs)))
```

```python
from contextlib import ExitStack

import concourse.bass as bass
from concourse import mybir

ALU = mybir.AluOpType
ACT = mybir.ActivationFunctionType
AX_X = mybir.AxisListType.X
F32 = mybir.dt.float32
F32R = mybir.dt.float32r

P = 128
LN_EPS = 1e-5
POOL_WINDOWS = (2, 4, 8, 16)
RAW = 2
SLOTS = 6
BLOCKS = 8


class Signal:

    def __init__(self, sem):
        self.sem, self.n = sem, 0

    def on(self, ins):
        ins.then_inc(self.sem, 1)
        self.n += 1
        return self.n


def build(nc, x_prompt, x_sample, state_conv, state_pool, ln1_g, ln1_b, ffn1_wg, ffn1_wu, ffn1_wd,
          w_in, conv_w, pool_w, pool_scale, w_out, ln2_g, ln2_b, ffn2_wg, ffn2_wu, ffn2_wd,
          ln3_g, ln3_b, y_prompt, y_sample, conv_prompt, pool_prompt, conv_sample, pool_sample):
    depth, D, FF = ffn1_wg.shape
    T = x_prompt.shape[1]
    NS = x_sample.shape[0] * x_sample.shape[1]
    PS = state_pool.shape[2]
    CS = state_conv.shape[2]
    assert depth == 1 and x_prompt.shape[0] == 1 and x_sample.shape[1] == 1
    ALPHA = (2.0 * depth) ** 0.25
    N = T + NS
    H = N // 2
    HB = T - H
    K = D // P
    KF = FF // P
    G = len(POOL_WINDOWS)
    TT = T // P
    assert K == BLOCKS and KF == 22 and K == 2 * G and N % 4 == 0 and H <= 512
    DQ = [(0, 8), (8, 8), (16, KF - 16)]
    INPUT_BANK = (0, 2, 1, 3, 4, 5, 6, 7)
    EARLY = K - 2

    UP = [0, 124]
    DOWN = [UP[0] + 2 * KF, UP[1] + 2 * KF]
    MIX = DOWN[0] + 3 * K
    OUT = MIX + 12 * G
    assert OUT + K == UP[1]
    CHUNKS = DOWN[1] + 3 * K
    assert CHUNKS % SLOTS == 0

    with ExitStack() as ctx:
        def sb(name, shape, dt=F32):
            return ctx.enter_context(nc.sbuf_tensor(name, shape, dt))

        def sem(name):
            return ctx.enter_context(nc.semaphore(name))

        x32 = sb("x32", [P, K, N])
        xh = sb("xh", [P, K, N], F32R)
        xl = sb("xl", [P, K, N], F32R)
        raw = sb("raw", [P, RAW, BLOCKS, P])
        wh = sb("wh", [P, SLOTS, BLOCKS, P], F32R)
        wl = sb("wl", [P, SLOTS, BLOCKS, P], F32R)
        par = sb("par", [P, 10 * K])
        warm = sb("warm", [P, 1])
        ident = sb("ident", [P, P])
        ones_tile = sb("ones_tile", [P, P])
        ones_mean = sb("ones_mean", [P, P])
        conv_state = sb("conv_state", [P, K, NS, CS])
        pool_state = sb("pool_state", [P, G, NS, PS])
        scratch = sb("scratch", [P, 3 * N + 3 * H])
        gate = scratch[:, 0:2 * N].rearrange("p (s n) -> p s n", s=2)
        hid32 = scratch[:, 2 * N:3 * N]
        tile_sum = scratch[:, 0:N]
        square_sum = scratch[:, N:2 * N]
        square = scratch[:, 2 * N:3 * N]
        offset = scratch[:, 3 * N:3 * N + H]
        variance = scratch[:, 3 * N + H:3 * N + 2 * H]
        rstd = scratch[:, 3 * N + 2 * H:3 * N + 3 * H]

        def phase(*tensors):
            with ExitStack() as over:
                return [over.enter_context(nc.sbuf_tensor(name, shape, dt)) for name, shape, dt in tensors]

        xrow, srow, prow, csrow, psrow = phase(
            ("xrow", [P, TT, D], F32), ("srow", [NS, D], F32), ("prow", [10 * K, P], F32),
            ("csrow", [NS * CS, D], F32), ("psrow", [NS * PS, G * P], F32))
        hid = [None, None]
        hid[0] = phase(("hid1_hi", [P, KF, N], F32R), ("hid1_lo", [P, KF, N], F32R))
        WP = 16 + T
        (mh, ml, pext, psmp, win, q32, qh, ql, csb, uext, usmp, ymix, vmix, sga, sgp, yp, rcount, first,
         sampsum, utail, ptail, utrow, ptrow) = phase(
            ("mh", [P, K, N], F32R), ("ml", [P, K, N], F32R), ("pext", [P, WP], F32),
            ("psmp", [P, NS, 16], F32), ("win", [P, 2, WP], F32), ("q32", [P, N], F32),
            ("qh", [P, N], F32R), ("ql", [P, N], F32R), ("csb", [P, N], F32), ("uext", [P, 2 + T], F32),
            ("usmp", [P, NS, 3], F32), ("ymix", [P, N], F32), ("vmix", [P, N], F32), ("sga", [P, N], F32),
            ("sgp", [P, N], F32), ("yp", [P, 2, N], F32), ("rcount", [P, 16], F32), ("first", [P, 16], F32),
            ("sampsum", [P, NS], F32), ("utail", [P, K, CS + NS], F32), ("ptail", [P, G, PS + NS], F32),
            ("utrow", [CS + NS, D], F32), ("ptrow", [PS + NS, G * P], F32))
        hid[1] = phase(("hid2_hi", [P, KF, N], F32R), ("hid2_lo", [P, KF, N], F32R))
        yrow, ysrow = phase(("yrow", [P, TT, D], F32), ("ysrow", [NS, D], F32))

        ps = ctx.enter_context(nc.psum_tensor("ps", [P, 8, 512], F32))

        def bank(pair, h):
            return ps[:, 2 * pair + h, 0:H]

        def pair_of(pair):
            return ps[:, 2 * pair:2 * pair + 2, 0:H]

        def two(ap):
            return ap.rearrange("p (h n) -> p h n", h=2)

        def half(ap, h):
            return ap[:, h * H:(h + 1) * H]

        rows_in = sem("rows_in")
        small_in = sem("small_in")
        const_ready = sem("const_ready")
        cols_made = sem("cols_made")
        cols_read = sem("cols_read")
        x_round = sem("x_round")
        x_ready = sem("x_ready")
        raw_in = [sem(f"raw_in{r}") for r in range(RAW)]
        hi_ready = sem("hi_ready")
        lo_ready = sem("lo_ready")
        w_used = sem("w_used")
        out_done = sem("out_done")

        class Ffn:
            def __init__(self, n):
                self.gate_on = sem(f"gate_on{n}")
                self.gated = sem(f"gated{n}")
                self.hid_made = sem(f"hid_made{n}")
                self.hid_round = sem(f"hid_round{n}")
                self.hid_ready = sem(f"hid_ready{n}")

        class Norm:
            def __init__(self, n):
                self.turn = sem(f"turn{n}")
                self.shift = sem(f"shift{n}")
                self.shifted = sem(f"shifted{n}")
                self.half_done = sem(f"half_done{n}")
                self.centred = sem(f"centred{n}")
                self.squared = sem(f"squared{n}")
                self.c_sum = sem(f"c_sum{n}")
                self.q_sum = sem(f"q_sum{n}")
                self.stats = sem(f"stats{n}")
                self.chain = sem(f"chain{n}")
                self.rooted = sem(f"rooted{n}")
                self.minus = sem(f"minus{n}")
                self.scaled = sem(f"scaled{n}")
                self.affine = sem(f"affine{n}")
                self.round = sem(f"round{n}")
                self.ready = sem(f"ready{n}")

        ffn = [Ffn(1), Ffn(2)]
        norm = [Norm(1), Norm(2), Norm(3)]

        p_link = sem("p_link")
        q_made = sem("q_made")
        q_round = sem("q_round")
        q_ready = sem("q_ready")
        c_copied = sem("c_copied")
        u_made = sem("u_made")
        ya_made = sem("ya_made")
        sga_made = sem("sga_made")
        sgp_made = sem("sgp_made")
        yp_copied = sem("yp_copied")
        a_gated = sem("a_gated")
        p_gated = sem("p_gated")
        m_made = sem("m_made")
        m_round = sem("m_round")
        m_ready = sem("m_ready")
        tails_turned = sem("tails_turned")
        tails_copied = sem("tails_copied")
        tails_out = sem("tails_out")
        y_turned = sem("y_turned")
        y_copied = [sem("y_copied_act"), sem("y_copied_dve")]

        def blocks(w):
            return w[0].rearrange("(k p) n -> p k n", p=P)

        wg_v, wu_v, wd_v = ([blocks(a), blocks(b)] for a, b in (
            (ffn1_wg, ffn2_wg), (ffn1_wu, ffn2_wu), (ffn1_wd, ffn2_wd)))
        win_v, wout_v = blocks(w_in), blocks(w_out)
        C_AT, B_AT, H_AT, P_AT = 0, K, 2 * K, 3 * K
        GA_AT, GP_AT = P_AT + G, P_AT + G + K

        UP_LOOP = (KF - 4) // 6

        def up_tiles(eng, body):
            for f in (0, 1):
                body(f, f)
            with eng.Fori(0, UP_LOOP) as i:
                for j in range(6):
                    body(i * 6 + (2 + j), 2 + j)
            for f in (KF - 2, KF - 1):
                body(f, f)

        block = ctx.enter_context(nc.Block())

        @block.sync
        def _(sp):
            def load(c, place, src, wait=True):
                n = src.shape[1]
                if wait:
                    sp.wait_ge(lo_ready, c - (RAW - 1))
                sp.dma_start(raw[:, place % RAW, 0:n, :], src).then_inc(raw_in[place % RAW], 16)

            for t in range(TT):
                sp.dma_start(xrow[:, t, :], x_prompt[0, t * P:(t + 1) * P, :]).then_inc(rows_in, 16)

            def column(v, f):
                return v[:, :, bass.ds(f * P, P)]

            for n in range(2):
                def up(f, place):
                    c, cs = 2 * f + UP[n], 2 * place + UP[n]
                    first_chunks = n == 0 and isinstance(f, int) and f == 0
                    load(c, cs, column(wg_v[n], f), not first_chunks)
                    load(c + 1, cs + 1, column(wu_v[n], f), not first_chunks)
                up_tiles(sp, up)
                with sp.Fori(0, K // 2) as i:
                    for j in range(2):
                        for q, (k0, nk) in enumerate(DQ):
                            c = i * 6 + (DOWN[n] + 3 * j + q)
                            load(c, DOWN[n] + 3 * j + q, wd_v[n][:, k0:k0 + nk, bass.ds(i * (2 * P) + j * P, P)])
                if n == 1:
                    break
                with sp.Fori(0, G) as g:
                    def mix(place, v):
                        load(g * 12 + (MIX + place), MIX + place, v)
                    mix(0, column(win_v, g + P_AT))
                    for j in range(2):
                        at = 1 if j == 0 else 7
                        mix(at, column(win_v, g * 2 + (C_AT + j)))
                        mix(at + 1, column(win_v, g * 2 + (H_AT + j)))
                        mix(at + 2, column(win_v, g * 2 + (B_AT + j)))
                        if j == 0:
                            mix(4, pool_w[0, bass.ds(g, 1), :, :].rearrange("g p (j n) -> p (g j) n", n=P))
                            at = 2
                        mix(at + 3, column(win_v, g * 2 + (GA_AT + j)))
                        mix(at + 4, column(win_v, g * 2 + (GP_AT + j)))
                for d in range(K):
                    load(OUT + d, OUT + d, column(wout_v, d))

            for t in range(TT):
                sp.wait_ge(y_copied[0], t + 1)
                sp.wait_ge(y_copied[1], t + 1)
                sp.dma_start(y_prompt[0, t * P:(t + 1) * P, :], yrow[:, t, :]).then_inc(out_done, 16)
            sp.wait_ge(y_copied[0], TT + 1)
            sp.wait_ge(y_copied[1], TT + 1)
            sp.dma_start(y_sample.rearrange("b t d -> (b t) d"), ysrow[:]).then_inc(out_done, 16)
            sp.wait_ge(out_done, 16 * (TT + 1 + 2))
            sp.wait_ge(tails_out, 16 * 4)

        @block.gpsimd
        def _(pool):
            made = Signal(const_ready)
            made.on(nc.gpsimd.memset(ident[:], 0.0))
            pool.wait_ge(const_ready, 1)
            made.on(nc.gpsimd.affine_select(out=ident[:], in_=ident[:], compare_op=ALU.not_equal, fill=1.0,
                                            base=0, pattern=[[-1, P]], channel_multiplier=1))
            made.on(nc.gpsimd.memset(ones_tile[:], 1.0 / P))
            made.on(nc.gpsimd.memset(ones_mean[:], 1.0 / D))
            assert made.n == 4
            with pool.Fori(0, CHUNKS // SLOTS) as i:
                for j in range(SLOTS):
                    pool.wait_ge(hi_ready, i * SLOTS + (j + 1))
                    nc.gpsimd.tensor_tensor(wl[:, j], raw[:, j % RAW], wh[:, j].bitcast(F32),
                                            ALU.subtract).then_inc(lo_ready, 1)

        @block.scalar
        def _(act):
            def copy(out, in_):
                return nc.scalar.activation(out, in_, ACT.Copy)

            def round_chunk(c, place, free=True):
                if isinstance(c, int) and c >= CHUNKS:
                    return
                if free:
                    act.wait_ge(w_used, c - (SLOTS - 1))
                if isinstance(c, int):
                    act.wait_ge(raw_in[place % RAW], 16 * (c // RAW + 1))
                else:
                    act.wait_ge(raw_in[place % RAW], c * 8 + (16 - 8 * (place % RAW)))
                copy(wh[:, place % SLOTS], raw[:, place % RAW]).then_inc(hi_ready, 1)

            act.dma_start(srow[:], x_sample.rearrange("b t d -> (b t) d")).then_inc(small_in, 16)
            for n, v in enumerate((ln1_g, ln1_b, ln2_g, ln2_b, ln3_g, ln3_b, pool_scale)):
                act.dma_start(prow[n * K:(n + 1) * K, :], v[0].rearrange("(k p) -> k p", p=P)).then_inc(small_in, 16)
            act.dma_start(prow[7 * K:10 * K, :], conv_w[0].rearrange("w (k p) -> (w k) p", p=P)).then_inc(small_in, 16)
            act.dma_start(csrow[:], state_conv[0].rearrange("b s d -> (b s) d")).then_inc(small_in, 16)
            act.dma_start(psrow[:], state_pool[0].rearrange("b s d -> (b s) d")).then_inc(small_in, 16)
            act.dma_start(conv_sample[0, :, 0:CS - 1, :], state_conv[0, :, 1:CS, :]).then_inc(out_done, 16)
            act.dma_start(pool_sample[0, :, 0:PS - 1, :], state_pool[0, :, 1:PS, :]).then_inc(out_done, 16)

            round_chunk(0, 0, False)
            round_chunk(1, 1, False)
            for k in range(K):
                act.wait_ge(cols_read, 5 + k)
                copy(xh[:, k, :], x32[:, k, :]).then_inc(x_round, 1)
                if k % 2 == 1:
                    round_chunk(2 + k // 2, 2 + k // 2, False)

            def square_tile(n, m, t=None, h=None):
                s = norm[n]
                act.wait_ge(s.centred, m + 1)
                if m == 0:
                    nc.scalar.activation(square_sum, x32[:, 0, :], ACT.Square).then_inc(s.squared, 1)
                    return
                if m >= 2:
                    act.wait_ge(s.q_sum, m - 1)
                if h is None:
                    nc.scalar.activation(square, x32[:, m, :], ACT.Square).then_inc(s.squared, 1)
                else:
                    nc.scalar.activation(half(square, h), half(x32[:, t, :], h), ACT.Square).then_inc(s.squared, 1)

            def ffn_steps(n):
                s = ffn[n]

                def up(f, place):
                    c, cs = 2 * f + UP[n], 2 * place + UP[n]
                    pair = 2 * (place % 2)
                    act.wait_ge(w_used, c + 1)
                    if not (isinstance(f, int) and f < 2):
                        act.wait_ge(s.gated, f - 1)
                    nc.scalar.activation(two(gate[:, place % 2, :]), pair_of(pair),
                                         ACT.Sigmoid).then_inc(s.gate_on, 1)
                    round_chunk(c + SLOTS, cs + SLOTS)
                    round_chunk(c + 1 + SLOTS, cs + 1 + SLOTS)
                    act.wait_ge(s.hid_made, f + 1)
                    if n == 1 and isinstance(f, int) and f == 0:
                        act.wait_ge(tails_out, 64)
                    copy(hid[n][0][:, bass.ds(f, 1), :].rearrange("p a n -> p (a n)"), hid32).then_inc(s.hid_round, 1)
                up_tiles(act, up)
                for t in range(EARLY):
                    for q in range(3):
                        c = DOWN[n] + 3 * t + q + SLOTS
                        round_chunk(c, c)
                    square_tile(2 * n, t)

            def norm_steps(n, rounds, last=False):
                s = norm[n]

                def chunk_at(place):
                    if place in rounds:
                        round_chunk(rounds[place], rounds[place])

                for h in range(2):
                    if h == 0:
                        square_tile(n, EARLY, EARLY, 0)
                    square_tile(n, EARLY + 2 * h + 1, EARLY + 1, h)
                    if h == 0:
                        nc.scalar.activation(warm[:], ones_tile[:, 0:1], ACT.Sqrt)
                        chunk_at("before root")
                    act.wait_ge(s.chain, 8 * h + 4)
                    nc.scalar.activation(rstd, variance, ACT.Sqrt).then_inc(s.rooted, 1)
                    if h == 0:
                        chunk_at("after root")
                        square_tile(n, EARLY + 2, EARLY, 1)
                        chunk_at("after square")
                    for kk in range(K // 2):
                        if not last:
                            act.wait_ge(s.affine, 4 * h + kk + 1)
                            copy(xh[:, 2 * kk:2 * kk + 2, h * H:(h + 1) * H],
                                 x32[:, 2 * kk:2 * kk + 2, h * H:(h + 1) * H]).then_inc(s.round, 1)
                        if h == 0:
                            chunk_at(kk)
                if not last:
                    nc.scalar.activation(warm[:], ones_tile[:, 0:1], ACT.Sigmoid)

            ffn_steps(0)
            norm_steps(0, dict(zip(("before root", "after root", "after square", 0, 2, 3),
                                   range(MIX, MIX + SLOTS))))

            def reused(used, times):
                if not (isinstance(times, int) and times == 0):
                    act.wait_ge(used, times)

            def mix_group(g):
                def next_chunk(j):
                    round_chunk(g * 12 + (MIX + j + SLOTS), MIX + j + SLOTS)

                def copy_c(j, at):
                    act.wait_ge(w_used, g * 12 + (MIX + at + 1))
                    reused(u_made, g * 2 + j)
                    copy(two(csb[:]), pair_of(1 if j == 0 else 0)).then_inc(c_copied, 1)

                def gates(j, at):
                    act.wait_ge(w_used, g * 12 + (MIX + at + 1))
                    reused(a_gated, g * 2 + j)
                    nc.scalar.activation(two(sga[:]), pair_of(2 if j == 0 else 3), ACT.Sigmoid).then_inc(sga_made, 1)
                    next_chunk(at)
                    act.wait_ge(w_used, g * 12 + (MIX + at + 2))
                    reused(p_gated, g * 2 + j)
                    nc.scalar.activation(two(sgp[:]), pair_of(3 if j == 0 else 1), ACT.Sigmoid).then_inc(sgp_made, 1)
                    next_chunk(at + 1)
                    act.wait_ge(m_made, g * 2 + (j + 1))
                    copy(mh[:, bass.ds(g * 2 + j, 1), :].rearrange("p a n -> p (a n)"), ymix[:]).then_inc(m_round, 1)

                next_chunk(0)
                copy_c(0, 1)
                next_chunk(1)
                act.wait_ge(q_made, g + 1)
                copy(qh[:], q32[:]).then_inc(q_round, 1)
                next_chunk(2)
                next_chunk(3)
                act.wait_ge(w_used, g * 12 + (MIX + 5))
                reused(p_gated, g * 2)
                for j in range(2):
                    copy(two(yp[:, j, :]), pair_of(j)).then_inc(yp_copied, 1)
                next_chunk(4)
                gates(0, 5)
                copy_c(1, 7)
                next_chunk(7)
                next_chunk(8)
                next_chunk(9)
                gates(1, 10)

            mix_group(0)
            with act.Fori(1, G) as g:
                mix_group(g)

            for t in range(EARLY):
                round_chunk(OUT + t + SLOTS, OUT + t + SLOTS)
                square_tile(1, t)
                if t == 3:
                    act.wait_ge(tails_turned, 1)
                    copied = Signal(tails_copied)
                    for b in range(2):
                        copied.on(copy(utrow[:, b * 512:(b + 1) * 512], ps[0:CS + NS, 6 + b, :]))
                    copied.on(copy(ptrow[:], ps[0:PS + NS, 4, :]))
                    act.wait_ge(tails_copied, 3)
                    act.dma_start(conv_prompt[0, 0], utrow[0:CS, :]).then_inc(tails_out, 16)
                    act.dma_start(conv_sample[0, :, CS - 1, :], utrow[CS:CS + NS, :]).then_inc(tails_out, 16)
                    act.dma_start(pool_prompt[0, 0], ptrow[0:PS, :]).then_inc(tails_out, 16)
                    act.dma_start(pool_sample[0, :, PS - 1, :], ptrow[PS:PS + NS, :]).then_inc(tails_out, 16)
            norm_steps(1, {2: UP[1] + 4, 3: UP[1] + 5})
            ffn_steps(1)
            norm_steps(2, {}, last=True)
            for t in range(TT + 1):
                act.wait_ge(y_turned, t + 1)
                if t < TT:
                    copy(yrow[:, t, 0:512], ps[:, 2 * t, :]).then_inc(y_copied[0], 1)
                else:
                    copy(ysrow[:, 0:512], ps[0:NS, 0, :]).then_inc(y_copied[0], 1)

        @block.vector
        def _(dve):
            tt, ts, stt = nc.vector.tensor_tensor, nc.vector.tensor_scalar, nc.vector.scalar_tensor_tensor
            copy = nc.vector.tensor_copy

            read = Signal(cols_read)
            dve.wait_ge(cols_made, 1)
            read.on(copy(x32[:, :, T:N], ps[:, 7, 0:K * NS].rearrange("p (k n) -> p k n", k=K)))
            read.on(copy(par[:], ps[:, 7, 128:128 + 10 * K]))
            read.on(copy(conv_state[:].rearrange("p k b s -> p (k b s)"), ps[:, 7, 208:208 + K * NS * CS]))
            dve.wait_ge(cols_made, 2)
            read.on(copy(pool_state[:].rearrange("p g b s -> p (g b s)"), ps[:, 6, 0:G * NS * PS]))

            def x_lo(k):
                dve.wait_ge(x_round, k + 1)
                tt(xl[:, k, :], x32[:, k, :], xh[:, k, :].bitcast(F32), ALU.subtract).then_inc(x_ready, 1)
            for k in range(K):
                dve.wait_ge(cols_made, 3 + k)
                read.on(copy(x32[:, k, 0:T], ps[:, INPUT_BANK[k], :]))
                if k >= 1:
                    x_lo(k - 1)
            x_lo(K - 1)

            def up_steps(n):
                s = ffn[n]

                def up(f, place):
                    pair = 2 * (place % 2)
                    g = gate[:, place % 2, :]
                    dve.wait_ge(s.gate_on, f + 1)
                    tt(two(g), two(g), pair_of(pair), ALU.mult).then_inc(s.gated, 1)
                    dve.wait_ge(s.gated, f + 1)
                    dve.wait_ge(w_used, 2 * f + (UP[n] + 2))
                    tt(two(hid32), two(g), pair_of(pair + 1), ALU.mult).then_inc(s.hid_made, 1)
                    dve.wait_ge(s.hid_made, f + 1)
                    dve.wait_ge(s.hid_round, f + 1)
                    one = bass.ds(f, 1)
                    tt(hid[n][1][:, one, :].rearrange("p a n -> p (a n)"), hid32,
                       hid[n][0][:, one, :].rearrange("p a n -> p (a n)").bitcast(F32),
                       ALU.subtract).then_inc(s.hid_ready, 1)
                up_tiles(dve, up)

            def scale_residual(n):
                dve.wait_ge(x_ready, K) if n == 0 else dve.wait_ge(norm[n - 1].ready, K)
                for k in (0, K // 2):
                    ts(x32[:, k:k + K // 2], x32[:, k:k + K // 2], ALPHA, None, ALU.mult).then_inc(norm[n].turn, 1)

            def norm_steps(n, start, per, weight, g_at, b_at, last=False):
                s = norm[n]
                dve.wait_ge(s.turn, 2)
                dve.wait_ge(w_used, start + per)
                y = two(x32[:, 0, :])
                stt(y, pair_of(0), weight, y, ALU.mult, ALU.add).then_inc(s.turn, 1)
                dve.wait_ge(s.turn, 3)
                dve.wait_ge(s.shift, 2)
                tt(y, y, pair_of(2), ALU.subtract).then_inc(s.centred, 1)
                for t in range(1, K):
                    y = two(x32[:, t, :])
                    tt(y, y, pair_of(2), ALU.subtract).then_inc(s.shifted, 1)

                def add(m, c, h=None):
                    part = (lambda a: a) if h is None else (lambda a: half(a, h))
                    dve.wait_ge(s.centred, m + 1)
                    if m >= 2:
                        dve.wait_ge(s.c_sum, m - 1)
                    tt(part(tile_sum), part(tile_sum) if m >= 2 else x32[:, 0, :], c, ALU.add).then_inc(s.c_sum, 1)
                    dve.wait_ge(s.squared, m + 1)
                    if m >= 2:
                        dve.wait_ge(s.q_sum, m - 1)
                    tt(part(square_sum), part(square_sum), part(square), ALU.add).then_inc(s.q_sum, 1)

                for t in range(1, EARLY):
                    dve.wait_ge(w_used, start + per * (t + 1))
                    dve.wait_ge(s.shifted, t)
                    y = two(x32[:, t, :])
                    stt(y, pair_of(t % 2), weight, y, ALU.mult, ALU.add).then_inc(s.centred, 1)
                    add(t, x32[:, t, :])

                def tile_half(m, t, h):
                    if h == 0:
                        dve.wait_ge(s.half_done, t - EARLY + 1)
                    else:
                        dve.wait_ge(w_used, start + per * (t + 1))
                    dve.wait_ge(s.shifted, t)
                    y = half(x32[:, t, :], h)
                    stt(y, bank(t % 2, h), weight, y, ALU.mult, ALU.add).then_inc(s.centred, 1)
                    add(m, y, h)

                def normalise(h):
                    link = Signal(s.chain)
                    link.n = 8 * h

                    def then(ins):
                        dve.wait_ge(s.chain, link.on(ins))
                    var, t = variance, half(square, h)
                    dve.wait_ge(s.stats, h + 1)
                    then(copy(offset, bank(3, h)))
                    then(tt(var, offset, offset, ALU.mult))
                    then(tt(var, bank(2, h), var, ALU.subtract))
                    then(ts(var, var, 0.0, LN_EPS, ALU.max, ALU.add))
                    dve.wait_ge(s.rooted, h + 1)
                    then(nc.vector.reciprocal(rstd, rstd))
                    then(tt(t, rstd, rstd, ALU.mult))
                    then(stt(t, t, -0.5, var, ALU.mult, ALU.mult))
                    then(stt(rstd, t, 1.5, rstd, ALU.add, ALU.mult))
                    assert link.n == 8 * (h + 1)
                    if h == 0:
                        tile_half(EARLY + 2, EARLY, 1)

                    def tiles(a, kk):
                        return a[:, 2 * kk:2 * kk + 2, h * H:(h + 1) * H]

                    def minus(kk):
                        v = tiles(x32, kk)
                        tt(v, v, offset.unsqueeze(1).broadcast_to([P, 2, H]), ALU.subtract).then_inc(s.minus, 1)

                    minus(0)
                    for kk in range(K // 2):
                        v = tiles(x32, kk)
                        dve.wait_ge(s.minus, 4 * h + kk + 1)
                        tt(v, v, rstd.unsqueeze(1).broadcast_to([P, 2, H]), ALU.mult).then_inc(s.scaled, 1)
                        if kk + 1 < K // 2:
                            minus(kk + 1)
                        dve.wait_ge(s.scaled, 4 * h + kk + 1)
                        for k in (2 * kk, 2 * kk + 1):
                            v = half(x32[:, k, :], h)
                            ins = ts(v, v, par[:, g_at + k:g_at + k + 1], par[:, b_at + k:b_at + k + 1],
                                     ALU.mult, ALU.add)
                        ins.then_inc(s.affine, 1)
                    if not last:
                        for kk in range(K // 2):
                            dve.wait_ge(s.round, 4 * h + kk + 1)
                            tt(tiles(xl, kk), tiles(x32, kk), tiles(xh, kk).bitcast(F32),
                               ALU.subtract).then_inc(s.ready, 1)

                tile_half(EARLY, EARLY, 0)
                tile_half(EARLY + 1, EARLY + 1, 0)
                normalise(0)
                tile_half(EARLY + 3, EARLY + 1, 1)
                normalise(1)

            scale_residual(0)
            up_steps(0)
            norm_steps(0, DOWN[0], 3, 0.5, 0, K)

            scale_residual(1)
            link = Signal(p_link)

            def then(ins):
                dve.wait_ge(p_link, link.on(ins))

            then(nc.vector.memset(pext[:, 0:16], 0.0))
            then(nc.vector.memset(uext[:, 0:2], 0.0))
            for i in range(15):
                then(nc.vector.memset(rcount[:, i:i + 1], 1.0 / (i + 1)))
            for g, w in enumerate(POOL_WINDOWS):
                base = MIX + 12 * g
                dve.wait_ge(w_used, base + 1)
                link.on(copy(psmp[:, :, 0:PS], pool_state[:, g]))
                link.on(copy(pext[:, 16:16 + H], bank(0, 0)))
                link.on(copy(psmp[:, :, PS], bank(0, 1)[:, HB:H]))
                then(copy(pext[:, 16 + H:16 + T], bank(0, 1)[:, 0:HB]))
                link.on(copy(ptail[:, g, 0:PS], pext[:, 16 + T - PS:16 + T]))
                link.on(copy(ptail[:, g, PS:PS + NS], psmp[:, :, PS]))
                src = pext[:]
                level = 0
                while (1 << level) < w:
                    s, lo = 1 << level, 2 * (1 << level) - 1
                    dst = win[:, level % 2, :]
                    then(tt(dst[:, lo:WP], src[:, lo:WP], src[:, lo - s:WP - s], ALU.add))
                    src, level = dst, level + 1
                then(nc.vector.tensor_reduce(sampsum[:], psmp[:, :, PS + 1 - w:PS + 1], AX_X, ALU.add))
                then(tt(first[:, 0:w - 1], src[:, 16:16 + w - 1], rcount[:, 0:w - 1], ALU.mult))
                link.on(stt(q32[:, w - 1:T], src[:, 16 + w - 1:WP], 1.0 / w, pext[:, 16 + w - 1:WP],
                            ALU.mult, ALU.subtract))
                link.on(stt(q32[:, T:N], sampsum[:], 1.0 / w, psmp[:, :, PS], ALU.mult, ALU.subtract))
                dve.wait_ge(p_link, link.n)
                tt(q32[:, 0:w - 1], first[:, 0:w - 1], pext[:, 16:16 + w - 1], ALU.subtract).then_inc(q_made, 1)
                dve.wait_ge(q_made, g + 1)
                dve.wait_ge(q_round, g + 1)
                tt(ql[:], q32[:], qh[:].bitcast(F32), ALU.subtract).then_inc(q_ready, 1)
                for j in range(2):
                    t = 2 * g + j
                    at = base + (1 if j == 0 else 7)
                    c_pair, h_pair, b_pair = ((1, 2, 3), (0, 1, 2))[j]
                    dve.wait_ge(w_used, at + 2)
                    dve.wait_ge(c_copied, t + 1)
                    link.on(copy(usmp[:, :, 0:CS], conv_state[:, t]))
                    link.on(tt(uext[:, 2:2 + H], csb[:, 0:H], bank(h_pair, 0), ALU.mult))
                    then(tt(usmp[:, :, CS], csb[:, T:N], bank(h_pair, 1)[:, HB:H], ALU.mult))
                    tt(uext[:, 2 + H:2 + T], csb[:, H:T], bank(h_pair, 1)[:, 0:HB], ALU.mult).then_inc(u_made, 1)
                    dve.wait_ge(u_made, t + 1)
                    link.on(copy(utail[:, t, 0:CS], uext[:, T:T + 2]))
                    link.on(copy(utail[:, t, CS:CS + NS], usmp[:, :, CS]))
                    for i in range(3):
                        wi = par[:, 7 * K + i * K + t:7 * K + i * K + t + 1]
                        parts = ((ymix[:, 0:T], uext[:, i:i + T]), (ymix[:, T:N], usmp[:, :, i]))
                        for y, u in parts:
                            if i == 0:
                                link.on(ts(y, u, wi, None, ALU.mult))
                            else:
                                link.on(stt(y, u, wi, y, ALU.mult, ALU.add))
                        dve.wait_ge(p_link, link.n)
                    dve.wait_ge(w_used, at + 3)
                    tt(two(ymix[:]), two(ymix[:]), pair_of(b_pair), ALU.mult).then_inc(ya_made, 1)
                    dve.wait_ge(ya_made, t + 1)
                    dve.wait_ge(sga_made, t + 1)
                    tt(ymix[:], ymix[:], sga[:], ALU.mult).then_inc(a_gated, 1)
                    dve.wait_ge(yp_copied, t + 1)
                    dve.wait_ge(sgp_made, t + 1)
                    stt(vmix[:], yp[:, j, :], par[:, 6 * K + t:6 * K + t + 1], sgp[:],
                        ALU.mult, ALU.mult).then_inc(p_gated, 1)
                    dve.wait_ge(a_gated, t + 1)
                    dve.wait_ge(p_gated, t + 1)
                    tt(ymix[:], ymix[:], vmix[:], ALU.add).then_inc(m_made, 1)
                    dve.wait_ge(m_made, t + 1)
                    dve.wait_ge(m_round, t + 1)
                    tt(ml[:, t, :], ymix[:], mh[:, t, :].bitcast(F32), ALU.subtract).then_inc(m_ready, 1)

            norm_steps(1, OUT, 1, 1.0, 2 * K, 3 * K)
            scale_residual(2)
            dve.wait_ge(tails_out, 64)
            up_steps(1)
            norm_steps(2, DOWN[1], 3, 0.5, 4 * K, 5 * K, last=True)
            for t in range(TT + 1):
                dve.wait_ge(y_turned, t + 1)
                if t < TT:
                    copy(yrow[:, t, 512:1024], ps[:, 2 * t + 1, :]).then_inc(y_copied[1], 1)
                else:
                    copy(ysrow[:, 512:1024], ps[0:NS, 1, :]).then_inc(y_copied[1], 1)

        @block.tensor
        def _(pe):
            mm = nc.tensor.matmul

            def run(out, blocks_, start=True, stop=True):
                todo = [b for b in blocks_ if not callable(b)]
                n = 0
                for b in blocks_:
                    if callable(b):
                        b()
                        continue
                    slot, k, vh, vl = b
                    n += 1
                    mm(out, wh[:, slot, k, :], vh, start=start and n == 1, stop=False)
                    mm(out, wh[:, slot, k, :], vl, start=False, stop=False)
                    ins = mm(out, wl[:, slot, k, :], vh, start=False, stop=stop and n == len(todo))
                return ins

            def x_blocks(slot, h):
                return [(slot, k, half(xh[:, k, :], h), half(xl[:, k, :], h)) for k in range(K)]

            def product(c, place, pair):
                pe.wait_ge(lo_ready, c + 1)
                for h in range(2):
                    ins = run(bank(pair, h), x_blocks(place % SLOTS, h))
                ins.then_inc(w_used, 1)

            def opening(c, hi, lo, groups, between=None, at=None):
                for h in range(2):
                    for js in groups:
                        for k in range(K):
                            hi(h, k)
                            for j in js:
                                if h == 0 and k == 0:
                                    pe.wait_ge(lo_ready, c + j + 1)
                                slot = (c + j) % SLOTS
                                mm(bank(j, h), wh[:, slot, k, :], half(xh[:, k, :], h), start=k == 0, stop=False)
                                mm(bank(j, h), wl[:, slot, k, :], half(xh[:, k, :], h), start=False, stop=False)
                            if h == 0 and js == groups[0] and k == at:
                                between()
                    for j in range(4):
                        for k in range(K):
                            if j == 0:
                                lo(h, k)
                            ins = mm(bank(j, h), wh[:, (c + j) % SLOTS, k, :], half(xl[:, k, :], h),
                                     start=False, stop=k == K - 1)
                        if h == 1:
                            ins.then_inc(w_used, 1)

            def norm_hi(n):
                def hi(h, k):
                    if k % 2 == 0:
                        pe.wait_ge(norm[n].round, 4 * h + k // 2 + 1)
                return hi

            def norm_lo(n):
                def lo(h, k):
                    if k % 2 == 0:
                        pe.wait_ge(norm[n].ready, 4 * h + k // 2 + 1)
                return lo

            def shift_sums(n):
                s = norm[n]
                pe.wait_ge(s.turn, 3)
                for h in range(2):
                    mm(bank(2, h), ones_tile[:], half(x32[:, 0, :], h), start=True, stop=True).then_inc(s.shift, 1)

            def stat_sums(n, h):
                s = norm[n]
                m = EARLY - 1 + 2 * (h + 1)
                pe.wait_ge(s.c_sum, m)
                mm(bank(3, h), ones_mean[:], half(tile_sum, h), start=True, stop=True)
                pe.wait_ge(s.q_sum, m)
                mm(bank(2, h), ones_mean[:], half(square_sum, h), start=True, stop=True).then_inc(s.stats, 1)

            def with_sums(blocks_, sums):
                return blocks_[:5] + [sums] + blocks_[5:]

            def closing(n, c, chunks_of, vectors):
                s = norm[n]
                for h in range(2):
                    for t in range(2):
                        if h == 0:
                            pe.wait_ge(s.centred, EARLY - 1 + t)
                        for q in range(chunks_of):
                            ch = c + chunks_of * t + q
                            if h == 0:
                                pe.wait_ge(lo_ready, ch + 1)
                            blocks_ = vectors(ch, q, h)
                            if h == 1 and t == 0 and q == 0:
                                blocks_ = with_sums(blocks_, lambda: stat_sums(n, 0))
                            ins = run(bank(t, h), blocks_, start=q == 0, stop=q == chunks_of - 1)
                            if h == 1:
                                ins.then_inc(w_used, 1)
                            elif q == chunks_of - 1:
                                ins.then_inc(s.half_done, 1)

            def hid_blocks(n, slot, q, h, wait=False):
                k0, nk = DQ[q]
                out = []
                for k in range(nk):
                    if wait:
                        out.append(lambda k=k: pe.wait_ge(ffn[n].hid_ready, k0 + k + 1))
                    out.append((slot, k, half(hid[n][0][:, k0 + k, :], h), half(hid[n][1][:, k0 + k, :], h)))
                return out

            def down(n, d, j, first):
                for h in range(2):
                    for q in range(3):
                        place = DOWN[n] + 3 * j + q
                        if h == 0:
                            pe.wait_ge(lo_ready, d * 3 + (DOWN[n] + q + 1))
                        blocks_ = hid_blocks(n, place % SLOTS, q, h, first and h == 0 and j == 0)
                        if first and h == 0 and j == 1 and q == 0:
                            blocks_ = with_sums(blocks_, lambda: shift_sums(2 * n))
                        ins = run(bank(j, h), blocks_, start=q == 0, stop=q == 2)
                        if h == 1:
                            ins.then_inc(w_used, 1)

            def ffn_steps(n, *how):
                s = ffn[n]

                def up(f, place):
                    if isinstance(f, int) and f < 2:
                        return
                    pair = 2 * (place % 2)
                    pe.wait_ge(s.gated, f - 1)
                    product(2 * f + UP[n], 2 * place + UP[n], pair)
                    pe.wait_ge(s.hid_made, f - 1)
                    product(2 * f + (UP[n] + 1), 2 * place + UP[n] + 1, pair + 1)
                opening(UP[n], *how)
                up_tiles(pe, up)
                pe.wait_ge(s.hid_made, KF - 1)
                pe.wait_ge(norm[2 * n].turn, 2)
                down(n, 0, 0, True)
                pe.wait_ge(s.hid_made, KF)
                down(n, 1, 1, True)
                with pe.Fori(0, EARLY // 2 - 1) as i:
                    for j in range(2):
                        pe.wait_ge(norm[2 * n].centred, i * 2 + (j + 1))
                        down(n, i * 2 + (2 + j), j, False)
                closing(2 * n, DOWN[n] + 18, 3, lambda ch, q, h: hid_blocks(n, ch % SLOTS, q, h))

            pe.wait_ge(const_ready, 4)
            pe.wait_ge(small_in, 16 * 11)
            for k in range(K):
                nc.tensor.transpose(ps[:, 7, k * NS:(k + 1) * NS], srow[:, k * P:(k + 1) * P], ident[0:NS, 0:NS])
                cw = NS * CS
                nc.tensor.transpose(ps[:, 7, 208 + k * cw:208 + (k + 1) * cw], csrow[:, k * P:(k + 1) * P],
                                    ident[0:cw, 0:cw])
            nc.tensor.transpose(ps[:, 7, 128:128 + 10 * K], prow[:], ident[0:10 * K, 0:10 * K]).then_inc(cols_made, 1)
            for g in range(G):
                pw = NS * PS
                ins = nc.tensor.transpose(ps[:, 6, g * pw:(g + 1) * pw], psrow[:, g * P:(g + 1) * P], ident[0:pw, 0:pw])
            ins.then_inc(cols_made, 1)
            pe.wait_ge(rows_in, 16 * TT)
            for k in range(K):
                if k == 6:
                    pe.wait_ge(cols_read, 4)
                for t in range(TT):
                    ins = nc.tensor.transpose(ps[:, INPUT_BANK[k], t * P:(t + 1) * P], xrow[:, t, k * P:(k + 1) * P], ident[:])
                ins.then_inc(cols_made, 1)

            ffn_steps(0, lambda h, k: pe.wait_ge(x_round, max(k + 1, 2)), lambda h, k: pe.wait_ge(x_ready, k + 1),
                      ((0, 1), (2, 3)))

            def mix_group(g, opened):
                def wproduct(at, pair):
                    product(g * 12 + (MIX + at), MIX + at, pair)

                if not opened:
                    pe.wait_ge(yp_copied, g * 2 - 1)
                    wproduct(0, 0)
                    pe.wait_ge(sgp_made, g * 2)
                    wproduct(1, 1)
                    pe.wait_ge(ya_made, g * 2)
                    wproduct(2, 2)
                    pe.wait_ge(sga_made, g * 2)
                    wproduct(3, 3)
                pe.wait_ge(lo_ready, g * 12 + (MIX + 5))
                pe.wait_ge(q_ready, g + 1)
                pe.wait_ge(c_copied, g * 2 + 1)
                slot = (MIX + 4) % SLOTS
                for j in range(2):
                    for h in range(2):
                        ins = run(bank(j, h), [(slot, j, half(qh[:], h), half(ql[:], h))])
                ins.then_inc(w_used, 1)
                pe.wait_ge(u_made, g * 2 + 1)
                wproduct(5, 2)
                pe.wait_ge(ya_made, g * 2 + 1)
                wproduct(6, 3)
                pe.wait_ge(yp_copied, g * 2 + 1)
                wproduct(7, 0)
                pe.wait_ge(yp_copied, g * 2 + 2)
                wproduct(8, 1)
                pe.wait_ge(sga_made, g * 2 + 1)
                wproduct(9, 2)
                pe.wait_ge(sgp_made, g * 2 + 1)
                wproduct(10, 3)
                pe.wait_ge(u_made, g * 2 + 2)
                wproduct(11, 1)

            opening(MIX, norm_hi(0), norm_lo(0), ((0, 1, 2, 3),), lambda: stat_sums(0, 1), 1)
            mix_group(0, True)
            with pe.Fori(1, G) as g:
                mix_group(g, False)

            def m_blocks(slot, h, ks=range(K)):
                return [(slot, k, half(mh[:, k, :], h), half(ml[:, k, :], h)) for k in ks]

            pe.wait_ge(c_copied, K)
            pe.wait_ge(lo_ready, OUT + 1)
            slot = OUT % SLOTS
            pe.wait_ge(m_ready, K - 1)
            for h in range(2):
                run(bank(0, h), m_blocks(slot, h, range(K - 1)), stop=False)
            pe.wait_ge(m_ready, K)
            for h in range(2):
                ins = run(bank(0, h), m_blocks(slot, h, [K - 1]), start=False)
            ins.then_inc(w_used, 1)
            for d in range(1, EARLY):
                if d == 1:
                    pe.wait_ge(sgp_made, K)
                else:
                    pe.wait_ge(norm[1].centred, d - 1)
                pe.wait_ge(lo_ready, OUT + d + 1)
                for h in range(2):
                    blocks_ = m_blocks((OUT + d) % SLOTS, h)
                    if d == 1 and h == 0:
                        blocks_ = with_sums(blocks_, lambda: shift_sums(1))
                    ins = run(bank(d % 2, h), blocks_)
                ins.then_inc(w_used, 1)
                if d == 3:
                    pe.wait_ge(norm[1].shifted, K - 1)
                    for g in range(G):
                        nc.tensor.transpose(ps[0:PS + NS, 4, g * P:(g + 1) * P], ptail[:, g, :], ident[:])
                    for t in range(K):
                        ins = nc.tensor.transpose(ps[0:CS + NS, 6 + t // 4, (t % 4) * P:(t % 4 + 1) * P],
                                                  utail[:, t, :], ident[:])
                    ins.then_inc(tails_turned, 1)
            pe.wait_ge(tails_copied, 3)
            closing(1, OUT + EARLY, 1, lambda ch, q, h: m_blocks(ch % SLOTS, h))

            ffn_steps(1, norm_hi(1), norm_lo(1), ((0, 1, 2, 3),), lambda: stat_sums(1, 1), 5)
            stat_sums(2, 1)

            for t in range(TT):
                pe.wait_ge(norm[2].affine, 4 if (t + 1) * P <= H else 8)
                for k in range(K):
                    ins = nc.tensor.transpose(ps[:, 2 * t + k // 4, (k % 4) * P:(k % 4 + 1) * P],
                                              x32[:, k, t * P:(t + 1) * P], ident[:])
                ins.then_inc(y_turned, 1)
            pe.wait_ge(y_copied[0], 1)
            pe.wait_ge(y_copied[1], 1)
            for k in range(K):
                ins = nc.tensor.transpose(ps[0:NS, k // 4, (k % 4) * P:(k % 4 + 1) * P], x32[:, k, T:N], ident[:])
            ins.then_inc(y_turned, 1)


_INS = ["x_prompt", "x_sample", "state_conv", "state_pool", "ln1_g", "ln1_b", "ffn1_wg", "ffn1_wu", "ffn1_wd",
        "w_in", "conv_w", "pool_w", "pool_scale", "w_out", "ln2_g", "ln2_b", "ffn2_wg", "ffn2_wu", "ffn2_wd",
        "ln3_g", "ln3_b"]


def kernel(**inputs):
    import numpy as _np
    import concourse.bacc as _bacc
    from concourse import mybir as _mybir
    from concourse.bass_utils import run_bass_kernel_spmd as _run

    nc = _bacc.Bacc("TRN2", target_bir_lowering=False, num_devices=1)
    arrays, args = {}, []
    for name in _INS:
        a = _np.ascontiguousarray(inputs[name])
        arrays[f"in_{name}_dram"] = a
        args.append(nc.dram_tensor(f"in_{name}_dram", a.shape, _mybir.dt.from_np(a.dtype), kind="ExternalInput").ap())
    depth, batch, cs, d = inputs["state_conv"].shape
    _, _, ps, dp = inputs["state_pool"].shape
    pb = inputs["x_prompt"].shape[0]
    outs = [inputs["x_prompt"].shape, inputs["x_sample"].shape, (depth, pb, cs, d), (depth, pb, ps, dp),
            (depth, batch, cs, d), (depth, batch, ps, dp)]
    for i, shape in enumerate(outs):
        args.append(nc.dram_tensor(f"out_{i}_dram", shape, F32, kind="ExternalOutput").ap())
    build(nc, *args)
    r = _run(nc, [arrays], core_ids=[0])
    return tuple(r.results[0][f"out_{i}_dram"] for i in range(len(outs)))
```

```python
from contextlib import ExitStack

import concourse.bass as bass
from concourse import mybir

ALU = mybir.AluOpType
ACT = mybir.ActivationFunctionType
AX_X = mybir.AxisListType.X
F32 = mybir.dt.float32
F32R = mybir.dt.float32r

P = 128
LN_EPS = 1e-5
POOL_WINDOWS = (2, 4, 8, 16)
RAW = 2
SLOTS = 6
BLOCKS = 8


class Signal:

    def __init__(self, sem):
        self.sem, self.n = sem, 0

    def on(self, ins):
        ins.then_inc(self.sem, 1)
        self.n += 1
        return self.n


def build(nc, x_prompt, x_sample, state_conv, state_pool, ln1_g, ln1_b, ffn1_wg, ffn1_wu, ffn1_wd,
          w_in, conv_w, pool_w, pool_scale, w_out, ln2_g, ln2_b, ffn2_wg, ffn2_wu, ffn2_wd,
          ln3_g, ln3_b, y_prompt, y_sample, conv_prompt, pool_prompt, conv_sample, pool_sample):
    depth, D, FF = ffn1_wg.shape
    T = x_prompt.shape[1]
    NS = x_sample.shape[0] * x_sample.shape[1]
    PS = state_pool.shape[2]
    CS = state_conv.shape[2]
    assert depth == 1 and x_prompt.shape[0] == 1 and x_sample.shape[1] == 1
    ALPHA = (2.0 * depth) ** 0.25
    N = T + NS
    H = N // 2
    HB = T - H
    K = D // P
    KF = FF // P
    G = len(POOL_WINDOWS)
    TT = T // P
    assert K == BLOCKS and KF == 22 and K == 2 * G and N % 4 == 0 and H <= 512
    DQ = [(0, 8), (8, 8), (16, KF - 16)]
    CLOSING = [2, 4, 2]
    EARLY = [K - c for c in CLOSING]
    BETWEEN = [{3: (0,), K // 2: (1,)}, {"offset": (0,), 2: (1,), 3: (2,), K // 2: (3,)}, {3: (0,), K // 2: (1,)}]
    ROW_BANK = (4, 6, 0, 2, 4)
    ROWS_A = H // P
    TURNED_LEFT = TT + 1
    assert D == 1024 and TT - ROWS_A == 2
    KEEP_WARM = 12
    WARM_UP = 16
    HQ = H // 4
    assert H % 4 == 0 and HQ <= P

    UP = [0, 124]
    DOWN = [UP[0] + 2 * KF, UP[1] + 2 * KF]
    MIX = DOWN[0] + 3 * K
    OUT = MIX + 12 * G
    assert OUT + K == UP[1]
    CHUNKS = DOWN[1] + 3 * K
    assert CHUNKS % SLOTS == 0

    with ExitStack() as ctx:
        def sb(name, shape, dt=F32):
            return ctx.enter_context(nc.sbuf_tensor(name, shape, dt))

        def sem(name):
            return ctx.enter_context(nc.semaphore(name))

        x32 = sb("x32", [P, K, N])
        xh = sb("xh", [P, K, N], F32R)
        xl = sb("xl", [P, K, N], F32R)
        raw = sb("raw", [P, RAW, BLOCKS, P])
        wh = sb("wh", [P, SLOTS, BLOCKS, P], F32R)
        wl = sb("wl", [P, SLOTS, BLOCKS, P], F32R)
        par = sb("par", [P, 10 * K])
        warm = sb("warm", [P, 1])
        ident = sb("ident", [P, P])
        ones_tile = sb("ones_tile", [P, P], F32R)
        ones_mean = sb("ones_mean", [P, P])
        rcount = sb("rcount", [P, 16])
        conv_state = sb("conv_state", [P, K, NS, CS])
        pool_state = sb("pool_state", [P, G, NS, PS])
        scratch = sb("scratch", [P, 3 * N])
        gate = scratch[:, 0:2 * N].rearrange("p (s n) -> p s n", s=2)
        hid32 = scratch[:, 2 * N:3 * N]
        tile_sum = scratch[:, 0:N]
        square_sum = scratch[:, N:2 * N]
        square = scratch[:, 2 * N:3 * N]
        offset = sb("offset", [P, H])
        rstd = sb("rstd", [P, H])
        means = sb("means", [HQ, 8])
        variance = sb("variance", [HQ, 4])
        root = sb("root", [HQ, 4])
        newton = sb("newton", [HQ, 4])

        def phase(*tensors):
            with ExitStack() as over:
                return [over.enter_context(nc.sbuf_tensor(name, shape, dt)) for name, shape, dt in tensors]

        xrow, srow, prow, csrow, psrow = phase(
            ("xrow", [P, TT, D], F32), ("srow", [NS, D], F32), ("prow", [10 * K, P], F32),
            ("csrow", [NS * CS, D], F32), ("psrow", [NS * PS, G * P], F32))
        hid = [None, None]
        hid[0] = phase(("hid1_hi", [P, KF, N], F32R), ("hid1_lo", [P, KF, N], F32R))
        WP = 16 + T
        (mh, ml, pext, psmp, win, q32, qh, ql, csb, uext, usmp, ymix, vmix, sga, sgp, yp, first,
         sampsum, utail, ptail, utrow, ptrow) = phase(
            ("mh", [P, K, N], F32R), ("ml", [P, K, N], F32R), ("pext", [P, WP], F32),
            ("psmp", [P, NS, 16], F32), ("win", [P, 2, WP], F32), ("q32", [P, N], F32),
            ("qh", [P, N], F32R), ("ql", [P, N], F32R), ("csb", [P, N], F32), ("uext", [P, 2 + T], F32),
            ("usmp", [P, NS, 3], F32), ("ymix", [P, N], F32), ("vmix", [P, N], F32), ("sga", [P, N], F32),
            ("sgp", [P, N], F32), ("yp", [P, 2, N], F32), ("first", [P, 16], F32),
            ("sampsum", [P, NS], F32), ("utail", [P, K, CS + NS], F32), ("ptail", [P, G, PS + NS], F32),
            ("utrow", [CS + NS, D], F32), ("ptrow", [PS + NS, G * P], F32))
        hid[1] = phase(("hid2_hi", [P, KF, N], F32R), ("hid2_lo", [P, KF, N], F32R))
        yrow, ysrow = phase(("yrow", [P, TT, D], F32), ("ysrow", [NS, D], F32))

        ps = ctx.enter_context(nc.psum_tensor("ps", [P, 8, 512], F32))

        def bank(pair, h):
            return ps[:, 2 * pair + h, 0:H]

        def pair_of(pair):
            return ps[:, 2 * pair:2 * pair + 2, 0:H]

        def two(ap):
            return ap.rearrange("p (h n) -> p h n", h=2)

        def half(ap, h):
            return ap[:, h * H:(h + 1) * H]

        def pair_tiles(ap, kk, h):
            return ap[:, 2 * kk:2 * kk + 2, h * H:(h + 1) * H]

        offset_twice = offset[:].unsqueeze(1).broadcast_to([P, 2, H])

        rows_in = [sem(f"rows_in{t}") for t in range(TT)]
        sample_in = sem("sample_in")
        small_in = sem("small_in")
        const_ready = sem("const_ready")
        cols_made = sem("cols_made")
        cols_read = sem("cols_read")
        x_round = [sem("x_round_even"), sem("x_round_odd")]
        x_read = [sem("x_read_even"), sem("x_read_odd")]
        x_ready = sem("x_ready")
        raw_in = [sem(f"raw_in{r}") for r in range(RAW)]
        hi_ready = sem("hi_ready")
        lo_ready = sem("lo_ready")
        w_used = sem("w_used")
        out_done = sem("out_done")

        class Ffn:
            def __init__(self, n):
                self.gate_on = sem(f"gate_on{n}")
                self.gated = sem(f"gated{n}")
                self.hid_made = sem(f"hid_made{n}")
                self.hid_round = sem(f"hid_round{n}")
                self.hid_ready = sem(f"hid_ready{n}")

        class Norm:
            def __init__(self, n):
                self.turn = sem(f"turn{n}")
                self.shift = sem(f"shift{n}")
                self.shifted = sem(f"shifted{n}")
                self.half_done = sem(f"half_done{n}")
                self.centred = sem(f"centred{n}")
                self.squared = sem(f"squared{n}")
                self.c_sum = sem(f"c_sum{n}")
                self.q_sum = sem(f"q_sum{n}")
                self.stats = sem(f"stats{n}")
                self.chain = sem(f"chain{n}")
                self.rooted = sem(f"rooted{n}")
                self.spread = sem(f"spread{n}")
                self.offset = sem(f"offset{n}")
                self.rstd = sem(f"rstd{n}")
                self.minus = sem(f"minus{n}")
                self.scaled = sem(f"scaled{n}")
                self.biased = sem(f"biased{n}")
                self.round = sem(f"round{n}")
                self.ready = sem(f"ready{n}")

        ffn = [Ffn(1), Ffn(2)]
        norm = [Norm(1), Norm(2), Norm(3)]

        pads_made = sem("pads_made")
        p_link = sem("p_link")
        q_made = sem("q_made")
        q_round = sem("q_round")
        q_ready = sem("q_ready")
        c_copied = sem("c_copied")
        u_made = sem("u_made")
        ya_made = sem("ya_made")
        sga_made = sem("sga_made")
        sgp_made = sem("sgp_made")
        yp_copied = sem("yp_copied")
        a_gated = sem("a_gated")
        p_gated = sem("p_gated")
        m_made = sem("m_made")
        m_round = sem("m_round")
        m_ready = sem("m_ready")
        tails_turned = sem("tails_turned")
        tails_copied = sem("tails_copied")
        tails_out = sem("tails_out")
        pool_minus = sem("pool_minus")
        y_turned = sem("y_turned")
        y_copied = [sem("y_copied_act"), sem("y_copied_dve")]

        def blocks(w):
            return w[0].rearrange("(k p) n -> p k n", p=P)

        wg_v, wu_v, wd_v = ([blocks(a), blocks(b)] for a, b in (
            (ffn1_wg, ffn2_wg), (ffn1_wu, ffn2_wu), (ffn1_wd, ffn2_wd)))
        win_v, wout_v = blocks(w_in), blocks(w_out)
        C_AT, B_AT, H_AT, P_AT = 0, K, 2 * K, 3 * K
        GA_AT, GP_AT = P_AT + G, P_AT + G + K

        UP_LOOP = (KF - 4) // 6

        def up_tiles(eng, body):
            for f in (0, 1):
                body(f, f)
            with eng.Fori(0, UP_LOOP) as i:
                for j in range(6):
                    body(i * 6 + (2 + j), 2 + j)
            for f in (KF - 2, KF - 1):
                body(f, f)

        block = ctx.enter_context(nc.Block())

        @block.sync
        def _(sp):
            def load(c, place, src, wait=True):
                n = src.shape[1]
                if wait:
                    sp.wait_ge(lo_ready, c - (RAW - 1))
                sp.dma_start(raw[:, place % RAW, 0:n, :], src).then_inc(raw_in[place % RAW], 16)

            for t in range(TT):
                sp.dma_start(xrow[:, t, :], x_prompt[0, t * P:(t + 1) * P, :]).then_inc(rows_in[t], 16)

            def column(v, f):
                return v[:, :, bass.ds(f * P, P)]

            load(0, 0, column(wg_v[0], 0), False)
            load(1, 1, column(wu_v[0], 0), False)
            for n, v in enumerate((ln1_g, ln1_b, ln2_g, ln2_b, ln3_g, ln3_b, pool_scale)):
                sp.dma_start(prow[n * K:(n + 1) * K, :], v[0].rearrange("(k p) -> k p", p=P)).then_inc(small_in, 16)
            sp.dma_start(prow[7 * K:10 * K, :], conv_w[0].rearrange("w (k p) -> (w k) p", p=P)).then_inc(small_in, 16)
            sp.dma_start(csrow[:], state_conv[0].rearrange("b s d -> (b s) d")).then_inc(small_in, 16)
            sp.dma_start(psrow[:], state_pool[0].rearrange("b s d -> (b s) d")).then_inc(small_in, 16)
            sp.dma_start(conv_sample[0, :, 0:CS - 1, :], state_conv[0, :, 1:CS, :]).then_inc(out_done, 16)
            sp.dma_start(pool_sample[0, :, 0:PS - 1, :], state_pool[0, :, 1:PS, :]).then_inc(out_done, 16)

            for n in range(2):
                def up(f, place):
                    c, cs = 2 * f + UP[n], 2 * place + UP[n]
                    if n == 0 and isinstance(f, int) and f == 0:
                        return
                    load(c, cs, column(wg_v[n], f))
                    load(c + 1, cs + 1, column(wu_v[n], f))
                up_tiles(sp, up)
                with sp.Fori(0, K // 2) as i:
                    for j in range(2):
                        for q, (k0, nk) in enumerate(DQ):
                            c = i * 6 + (DOWN[n] + 3 * j + q)
                            load(c, DOWN[n] + 3 * j + q, wd_v[n][:, k0:k0 + nk, bass.ds(i * (2 * P) + j * P, P)])
                if n == 1:
                    break
                with sp.Fori(0, G) as g:
                    def mix(place, v):
                        load(g * 12 + (MIX + place), MIX + place, v)
                    mix(0, column(win_v, g + P_AT))
                    for j in range(2):
                        at = 1 if j == 0 else 7
                        mix(at, column(win_v, g * 2 + (C_AT + j)))
                        mix(at + 1, column(win_v, g * 2 + (H_AT + j)))
                        mix(at + 2, column(win_v, g * 2 + (B_AT + j)))
                        if j == 0:
                            mix(4, pool_w[0, bass.ds(g, 1), :, :].rearrange("g p (j n) -> p (g j) n", n=P))
                            at = 2
                        mix(at + 3, column(win_v, g * 2 + (GA_AT + j)))
                        mix(at + 4, column(win_v, g * 2 + (GP_AT + j)))
                for d in range(K):
                    load(OUT + d, OUT + d, column(wout_v, d))

            for t in range(ROWS_A):
                sp.wait_ge(y_copied[0], 2 * t + 2)
                sp.dma_start(y_prompt[0, t * P:(t + 1) * P, :], yrow[:, t, :]).then_inc(out_done, 16)
            halves = ((TT - 2, 0, y_copied[1], 1), (TT - 1, 0, y_copied[1], 2),
                      (TT - 2, 1, y_copied[0], 2 * ROWS_A + 1), (TT - 1, 1, y_copied[1], 4))
            for t, side, copied, n in halves:
                cols = slice(side * 512, (side + 1) * 512)
                sp.wait_ge(copied, n)
                sp.dma_start(y_prompt[0, t * P:(t + 1) * P, cols], yrow[:, t, cols]).then_inc(out_done, 16)
            sp.wait_ge(y_copied[1], 3)
            sp.wait_ge(y_copied[0], 2 * ROWS_A + 2)
            sp.dma_start(y_sample.rearrange("b t d -> (b t) d"), ysrow[:]).then_inc(out_done, 16)
            sp.wait_ge(out_done, 16 * (ROWS_A + 2 * (TT - ROWS_A) + 1 + 2))
            sp.wait_ge(tails_out, 16 * 4)

        @block.gpsimd
        def _(pool):
            made = Signal(const_ready)
            made.on(nc.gpsimd.memset(ident[:], 0.0))
            pool.wait_ge(const_ready, 1)
            made.on(nc.gpsimd.affine_select(out=ident[:], in_=ident[:], compare_op=ALU.not_equal, fill=1.0,
                                            base=0, pattern=[[-1, P]], channel_multiplier=1))
            made.on(nc.gpsimd.memset(ones_mean[:], 1.0 / D))
            assert made.n == 3
            for i in range(max(POOL_WINDOWS) - 1):
                made.on(nc.gpsimd.memset(rcount[:, i:i + 1], 1.0 / (i + 1)))

            def split(c, place):
                pool.wait_ge(hi_ready, c + 1)
                nc.gpsimd.tensor_tensor(wl[:, place % SLOTS], raw[:, place % RAW],
                                        wh[:, place % SLOTS].bitcast(F32), ALU.subtract).then_inc(lo_ready, 1)

            def split_chunks(first, count):
                steps = count // SLOTS
                with pool.Fori(0, steps) as i:
                    for j in range(SLOTS):
                        split(i * SLOTS + (first + j), first + j)
                for c in range(first + steps * SLOTS, first + count):
                    split(c, c)

            def x_lo(n, h, chunks):
                for kk in range(K // 2):
                    for c in chunks.get(kk, ()):
                        split(c, c)
                    pool.wait_ge(norm[n].round, 4 * h + kk + 1)
                    nc.gpsimd.tensor_tensor(pair_tiles(xl, kk, h), pair_tiles(x32, kk, h),
                                            pair_tiles(xh, kk, h).bitcast(F32), ALU.subtract).then_inc(norm[n].ready, 1)

            split_chunks(0, MIX + 2)
            x_lo(0, 0, {1: (MIX + 2,)})
            x_lo(0, 1, {0: (MIX + 3, MIX + 4), 2: (MIX + 5,)})
            nc.gpsimd.memset(pext[:, 0:16], 0.0).then_inc(pads_made, 1)
            nc.gpsimd.memset(uext[:, 0:2], 0.0).then_inc(pads_made, 1)
            split_chunks(MIX + 6, UP[1] + 4 - (MIX + 6))
            x_lo(1, 0, {})
            x_lo(1, 1, {0: (UP[1] + 4,), 2: (UP[1] + 5,)})
            split_chunks(UP[1] + 6, CHUNKS - (UP[1] + 6))
            pool.wait_ge(norm[2].offset, 2)
            for kk in range(1, K // 2):
                nc.gpsimd.tensor_tensor(pair_tiles(x32, kk, 1), pair_tiles(x32, kk, 1), offset_twice,
                                        ALU.subtract).then_inc(pool_minus, 1)

        @block.scalar
        def _(act):
            def copy(out, in_):
                return nc.scalar.activation(out, in_, ACT.Copy)

            def round_chunk(c, place, free=True):
                if isinstance(c, int) and c >= CHUNKS:
                    return
                if free:
                    act.wait_ge(w_used, c - (SLOTS - 1))
                if isinstance(c, int):
                    act.wait_ge(raw_in[place % RAW], 16 * (c // RAW + 1))
                else:
                    act.wait_ge(raw_in[place % RAW], c * 8 + (16 - 8 * (place % RAW)))
                copy(wh[:, place % SLOTS], raw[:, place % RAW]).then_inc(hi_ready, 1)

            act.dma_start(srow[:], x_sample.rearrange("b t d -> (b t) d")).then_inc(sample_in, 16)
            act.wait_ge(cols_read, 1)
            copy(xh[:, :, T:N], x32[:, :, T:N]).then_inc(x_round[1], 1)

            def x_hi(k):
                act.wait_ge(cols_made, 2 + k)
                copy(xh[:, k, 0:T], ps[:, k, :]).then_inc(x_round[1], 1)

            def x_copy(k):
                copy(x32[:, k, 0:T], ps[:, k, :]).then_inc(x_read[1], 1)

            x_hi(1)
            x_copy(1)
            round_chunk(0, 0, False)
            for k in range(3, K, 2):
                x_hi(k)
            round_chunk(1, 1, False)
            for k in range(3, K, 2):
                x_copy(k)
            for c in range(2, SLOTS):
                round_chunk(c, c, False)

            def square_tile(n, m, t=None, h=None):
                s = norm[n]
                act.wait_ge(s.centred, m + 1)
                if m == 0:
                    nc.scalar.activation(square_sum, x32[:, 0, :], ACT.Square).then_inc(s.squared, 1)
                    return
                if m >= 2:
                    act.wait_ge(s.q_sum, m - 1)
                if h is None:
                    nc.scalar.activation(square, x32[:, m, :], ACT.Square).then_inc(s.squared, 1)
                else:
                    nc.scalar.activation(half(square, h), half(x32[:, t, :], h), ACT.Square).then_inc(s.squared, 1)

            def ffn_steps(n):
                s = ffn[n]

                def up(f, place):
                    c, cs = 2 * f + UP[n], 2 * place + UP[n]
                    pair = 2 * (place % 2)
                    act.wait_ge(w_used, c + 1)
                    if not (isinstance(f, int) and f < 2):
                        act.wait_ge(s.gated, f - 1)
                    nc.scalar.activation(two(gate[:, place % 2, :]), pair_of(pair),
                                         ACT.Sigmoid).then_inc(s.gate_on, 1)
                    round_chunk(c + SLOTS, cs + SLOTS)
                    round_chunk(c + 1 + SLOTS, cs + 1 + SLOTS)
                    act.wait_ge(s.hid_made, f + 1)
                    if n == 1 and isinstance(f, int) and f == 0:
                        act.wait_ge(tails_out, 64)
                    copy(hid[n][0][:, bass.ds(f, 1), :].rearrange("p a n -> p (a n)"), hid32).then_inc(s.hid_round, 1)
                up_tiles(act, up)
                for t in range(EARLY[2 * n]):
                    for q in range(3):
                        c = DOWN[n] + 3 * t + q + SLOTS
                        round_chunk(c, c)
                    square_tile(2 * n, t)

            def row_copies_of(t):
                act.wait_ge(y_turned, t + 1)
                for side in range(2):
                    copy(yrow[:, t, side * 512:(side + 1) * 512], ps[:, ROW_BANK[t] + side, :]).then_inc(y_copied[0], 1)

            def norm_steps(n, rounds, last=False):
                s = norm[n]

                def chunk_at(place):
                    for c in rounds.get(place, ()):
                        round_chunk(c, c)

                first = EARLY[n]

                def square_halves(h, tiles):
                    for i in tiles:
                        square_tile(n, first + CLOSING[n] * h + i, first + i, h)

                square_halves(0, range(CLOSING[n]))
                nc.scalar.activation(warm[:], ones_mean[:, 0:1], ACT.Sqrt)
                for h in range(2):
                    chunk_at((h, "root"))
                    act.wait_ge(s.chain, 8 * h + 4)
                    nc.scalar.activation(root[:], variance[:], ACT.Sqrt).then_inc(s.rooted, 1)
                    if h == 0:
                        chunk_at((h, "offset"))
                        square_halves(1, BETWEEN[n].get("offset", ()))
                    elif last:
                        row_copies_of(0)
                    act.wait_ge(s.spread, 2 * h + 1)
                    copy(offset[:], bank(1, h)).then_inc(s.offset, 1)
                    if last and h == 1:
                        row_copies_of(1)
                    for kk in range(K // 2):
                        chunk_at((h, kk))
                        if h == 0 and kk + 1 < K // 2:
                            square_halves(1, BETWEEN[n].get(kk + 1, ()))
                        act.wait_ge(s.scaled, 4 * h + kk + 1)
                        for k in (2 * kk, 2 * kk + 1):
                            b = par[:, (2 * n + 1) * K + k:(2 * n + 1) * K + k + 1]
                            v = half(x32[:, k, :], h)
                            ins = nc.scalar.activation(v, v, ACT.Identity, bias=b)
                        ins.then_inc(s.biased, 1)
                        if not last:
                            act.wait_ge(s.biased, 4 * h + kk + 1)
                            copy(pair_tiles(xh, kk, h), pair_tiles(x32, kk, h)).then_inc(s.round, 1)
                    if h == 0:
                        chunk_at((0, K // 2))
                        square_halves(1, BETWEEN[n].get(K // 2, ()))
                if not last:
                    nc.scalar.activation(warm[:], ones_mean[:, 0:1], ACT.Sigmoid)

            ffn_steps(0)
            norm_steps(0, {(0, "root"): (MIX,), (0, 0): (MIX + 1,), (0, 1): (MIX + 2,), (0, K // 2): (MIX + 3,),
                           (1, 0): (MIX + 4,), (1, 2): (MIX + 5,)})

            def reused(used, times):
                if not (isinstance(times, int) and times == 0):
                    act.wait_ge(used, times)

            def mix_group(g):
                def next_chunk(j):
                    round_chunk(g * 12 + (MIX + j + SLOTS), MIX + j + SLOTS)

                def copy_c(j, at):
                    act.wait_ge(w_used, g * 12 + (MIX + at + 1))
                    reused(u_made, g * 2 + j)
                    copy(two(csb[:]), pair_of(1 if j == 0 else 0)).then_inc(c_copied, 1)

                def gates(j, at):
                    act.wait_ge(w_used, g * 12 + (MIX + at + 1))
                    reused(a_gated, g * 2 + j)
                    nc.scalar.activation(two(sga[:]), pair_of(2 if j == 0 else 3), ACT.Sigmoid).then_inc(sga_made, 1)
                    next_chunk(at)
                    act.wait_ge(w_used, g * 12 + (MIX + at + 2))
                    reused(p_gated, g * 2 + j)
                    nc.scalar.activation(two(sgp[:]), pair_of(3 if j == 0 else 1), ACT.Sigmoid).then_inc(sgp_made, 1)
                    next_chunk(at + 1)
                    act.wait_ge(m_made, g * 2 + (j + 1))
                    copy(mh[:, bass.ds(g * 2 + j, 1), :].rearrange("p a n -> p (a n)"), ymix[:]).then_inc(m_round, 1)

                next_chunk(0)
                act.wait_ge(q_made, g + 1)
                copy(qh[:], q32[:]).then_inc(q_round, 1)
                copy_c(0, 1)
                next_chunk(1)
                next_chunk(2)
                next_chunk(3)
                act.wait_ge(w_used, g * 12 + (MIX + 5))
                reused(p_gated, g * 2)
                for j in range(2):
                    copy(two(yp[:, j, :]), pair_of(j)).then_inc(yp_copied, 1)
                next_chunk(4)
                gates(0, 5)
                copy_c(1, 7)
                next_chunk(7)
                next_chunk(8)
                next_chunk(9)
                gates(1, 10)

            mix_group(0)
            with act.Fori(1, G) as g:
                mix_group(g)

            for t in range(EARLY[1]):
                round_chunk(OUT + t + SLOTS, OUT + t + SLOTS)
                square_tile(1, t)
                if t == 2:
                    act.wait_ge(tails_turned, 1)
                    copied = Signal(tails_copied)
                    for b in range(2):
                        copied.on(copy(utrow[:, b * 512:(b + 1) * 512], ps[0:CS + NS, 6 + b, :]))
                    copied.on(copy(ptrow[:], ps[0:PS + NS, 4, :]))
                    act.wait_ge(tails_copied, 3)
                    act.dma_start(conv_prompt[0, 0], utrow[0:CS, :]).then_inc(tails_out, 16)
                    act.dma_start(conv_sample[0, :, CS - 1, :], utrow[CS:CS + NS, :]).then_inc(tails_out, 16)
                    act.dma_start(pool_prompt[0, 0], ptrow[0:PS, :]).then_inc(tails_out, 16)
                    act.dma_start(pool_sample[0, :, PS - 1, :], ptrow[PS:PS + NS, :]).then_inc(tails_out, 16)
            norm_steps(1, {(0, "offset"): (UP[1] + 2,), (0, 0): (UP[1] + 3,), (1, "root"): (UP[1] + 4,), (1, 2): (UP[1] + 5,)})
            ffn_steps(1)
            norm_steps(2, {}, last=True)
            act.wait_ge(y_turned, TURNED_LEFT + 1)
            copy(yrow[:, TT - 2, 512:1024], ps[:, ROW_BANK[TT - 2] + 1, :]).then_inc(y_copied[0], 1)
            act.wait_ge(y_turned, TURNED_LEFT + 3)
            copy(ysrow[:, 512:1024], ps[0:NS, ROW_BANK[TT] + 1, :]).then_inc(y_copied[0], 1)

        @block.vector
        def _(dve):
            tt, ts, stt = nc.vector.tensor_tensor, nc.vector.tensor_scalar, nc.vector.scalar_tensor_tensor
            copy = nc.vector.tensor_copy

            dve.wait_ge(const_ready, 3)
            ts(ones_tile[:], ones_mean[:], float(D // P), None, ALU.mult)
            read = Signal(cols_read)
            dve.wait_ge(cols_made, 1)
            read.on(copy(x32[:, :, T:N], ps[:, 7, 0:K * NS].rearrange("p (k n) -> p k n", k=K)))

            def x_hi(k):
                dve.wait_ge(cols_made, 2 + k)
                copy(xh[:, k, 0:T], ps[:, k, :]).then_inc(x_round[0], 1)

            def x_copy(k):
                copy(x32[:, k, 0:T], ps[:, k, :]).then_inc(x_read[0], 1)

            x_hi(0)
            x_copy(0)
            for k in range(2, K, 2):
                x_hi(k)
            for k in range(2, K, 2):
                x_copy(k)
            dve.wait_ge(x_round[1], 1)
            for k in range(K):
                dve.wait_ge(x_read[k % 2], k // 2 + 1)
                tt(xl[:, k, :], x32[:, k, :], xh[:, k, :].bitcast(F32), ALU.subtract).then_inc(x_ready, 1)

            dve.wait_ge(cols_made, K + 2)
            read.on(copy(par[:], ps[:, 7, 0:10 * K]))
            read.on(copy(conv_state[:].rearrange("p k b s -> p (k b s)"), ps[:, 7, 128:128 + K * NS * CS]))
            read.on(copy(pool_state[:].rearrange("p g b s -> p (g b s)"), ps[:, 6, 0:G * NS * PS]))

            def up_steps(n):
                s = ffn[n]

                def up(f, place):
                    pair = 2 * (place % 2)
                    g = gate[:, place % 2, :]
                    dve.wait_ge(s.gate_on, f + 1)
                    tt(two(g), two(g), pair_of(pair), ALU.mult).then_inc(s.gated, 1)
                    dve.wait_ge(s.gated, f + 1)
                    dve.wait_ge(w_used, 2 * f + (UP[n] + 2))
                    tt(two(hid32), two(g), pair_of(pair + 1), ALU.mult).then_inc(s.hid_made, 1)
                    dve.wait_ge(s.hid_made, f + 1)
                    dve.wait_ge(s.hid_round, f + 1)
                    one = bass.ds(f, 1)
                    tt(hid[n][1][:, one, :].rearrange("p a n -> p (a n)"), hid32,
                       hid[n][0][:, one, :].rearrange("p a n -> p (a n)").bitcast(F32),
                       ALU.subtract).then_inc(s.hid_ready, 1)
                    if isinstance(f, int) and f < 2:
                        scale_residual(2 * n, range(f * (K // 2), (f + 1) * (K // 2)))
                up_tiles(dve, up)

            def scale_residual(n, tiles):
                dve.wait_ge(x_ready, K) if n == 0 else dve.wait_ge(norm[n - 1].ready, K)
                for k in tiles:
                    ts(x32[:, k, :], x32[:, k, :], ALPHA, None, ALU.mult).then_inc(norm[n].turn, 1)

            def norm_steps(n, start, per, weight, last=False):
                s = norm[n]
                dve.wait_ge(s.turn, K)
                dve.wait_ge(w_used, start + per)
                y = two(x32[:, 0, :])
                stt(y, pair_of(0), weight, y, ALU.mult, ALU.add).then_inc(s.turn, 1)
                dve.wait_ge(s.turn, K + 1)
                copy(two(xh[:, 0, :]), y).then_inc(s.turn, 1)
                dve.wait_ge(s.shift, 2)
                tt(y, y, pair_of(2), ALU.subtract).then_inc(s.centred, 1)
                for t in range(1, K):
                    y = two(x32[:, t, :])
                    tt(y, y, pair_of(2), ALU.subtract).then_inc(s.shifted, 1)

                def add(m, c, h=None):
                    n_added = m - 1
                    part = (lambda a: a) if h is None else (lambda a: half(a, h))
                    dve.wait_ge(s.centred, m + 1)
                    if n_added:
                        dve.wait_ge(s.c_sum, n_added)
                    tt(part(tile_sum), part(tile_sum) if n_added else x32[:, 0, :], c, ALU.add).then_inc(s.c_sum, 1)
                    dve.wait_ge(s.squared, m + 1)
                    if n_added:
                        dve.wait_ge(s.q_sum, n_added)
                    tt(part(square_sum), part(square_sum), part(square), ALU.add).then_inc(s.q_sum, 1)

                first = EARLY[n]
                for t in range(1, first):
                    dve.wait_ge(w_used, start + per * (t + 1))
                    dve.wait_ge(s.shifted, t)
                    y = two(x32[:, t, :])
                    stt(y, pair_of(t % 2), weight, y, ALU.mult, ALU.add).then_inc(s.centred, 1)
                    add(t, x32[:, t, :])

                def tile_halves(h, tiles):
                    for i in tiles:
                        t = first + i
                        if h == 0:
                            dve.wait_ge(s.half_done, i + 1)
                        else:
                            dve.wait_ge(w_used, start + per * (t + 1))
                        dve.wait_ge(s.shifted, t)
                        y = half(x32[:, t, :], h)
                        stt(y, bank(i, h), weight, y, ALU.mult, ALU.add).then_inc(s.centred, 1)
                        add(first + CLOSING[n] * h + i, y, h)

                def normalise(h):
                    link = Signal(s.chain)
                    link.n = 8 * h

                    def then(ins):
                        dve.wait_ge(s.chain, link.on(ins))
                    var, t, r = variance[:], newton[:], root[:]
                    dve.wait_ge(s.stats, h + 1)
                    then(copy(means[:], ps[0:HQ, h, 0:8]))
                    then(tt(var, means[:, 0:4], means[:, 0:4], ALU.mult))
                    then(tt(var, means[:, 4:8], var, ALU.subtract))
                    then(ts(var, var, 0.0, LN_EPS, ALU.max, ALU.add))
                    dve.wait_ge(s.rooted, h + 1)
                    then(nc.vector.reciprocal(r, r))
                    then(tt(t, r, r, ALU.mult))
                    then(stt(t, t, -0.5, var, ALU.mult, ALU.mult))
                    then(stt(r, t, 1.5, r, ALU.add, ALU.mult))
                    assert link.n == 8 * (h + 1)

                    def minus(kk):
                        tt(pair_tiles(x32, kk, h), pair_tiles(x32, kk, h), offset_twice, ALU.subtract).then_inc(s.minus, 1)

                    between = BETWEEN[n] if h == 0 else {}
                    tile_halves(1, between.get("offset", ()))
                    dve.wait_ge(s.offset, h + 1)
                    minus(0)
                    dve.wait_ge(s.spread, 2 * h + 2)
                    copy(rstd[:], bank(0, h)).then_inc(s.rstd, 1)
                    dve.wait_ge(s.rstd, h + 1)
                    shared = last and h == 1
                    for kk in range(K // 2):
                        tile_halves(1, between.get(kk, ()))
                        if shared and kk:
                            dve.wait_ge(pool_minus, kk)
                        else:
                            dve.wait_ge(s.minus, 4 * h + kk + 1)
                        for k in (2 * kk, 2 * kk + 1):
                            v = half(x32[:, k, :], h)
                            ins = stt(v, v, par[:, 2 * n * K + k:2 * n * K + k + 1], rstd[:], ALU.mult, ALU.mult)
                        ins.then_inc(s.scaled, 1)
                        if kk + 1 < K // 2 and not shared:
                            minus(kk + 1)
                    tile_halves(1, between.get(K // 2, ()))

                tile_halves(0, range(CLOSING[n]))
                for h in range(2):
                    normalise(h)

            up_steps(0)
            norm_steps(0, DOWN[0], 3, 0.5)

            link = Signal(p_link)

            def then(ins):
                dve.wait_ge(p_link, link.on(ins))

            dve.wait_ge(const_ready, 3 + max(POOL_WINDOWS) - 1)
            dve.wait_ge(pads_made, 2)
            for g, w in enumerate(POOL_WINDOWS):
                base = MIX + 12 * g
                link.on(copy(psmp[:, :, 0:PS], pool_state[:, g]))
                dve.wait_ge(w_used, base + 1)
                link.on(copy(pext[:, 16:16 + H], bank(0, 0)))
                link.on(copy(psmp[:, :, PS], bank(0, 1)[:, HB:H]))
                then(copy(pext[:, 16 + H:16 + T], bank(0, 1)[:, 0:HB]))
                src = pext[:]
                level = 0
                while (1 << level) < w:
                    s, lo = 1 << level, 2 * (1 << level) - 1
                    dst = win[:, level % 2, :]
                    then(tt(dst[:, lo:WP], src[:, lo:WP], src[:, lo - s:WP - s], ALU.add))
                    src, level = dst, level + 1
                then(nc.vector.tensor_reduce(sampsum[:], psmp[:, :, PS + 1 - w:PS + 1], AX_X, ALU.add))
                then(tt(first[:, 0:w - 1], src[:, 16:16 + w - 1], rcount[:, 0:w - 1], ALU.mult))
                link.on(stt(q32[:, w - 1:T], src[:, 16 + w - 1:WP], 1.0 / w, pext[:, 16 + w - 1:WP],
                            ALU.mult, ALU.subtract))
                link.on(stt(q32[:, T:N], sampsum[:], 1.0 / w, psmp[:, :, PS], ALU.mult, ALU.subtract))
                dve.wait_ge(p_link, link.n)
                tt(q32[:, 0:w - 1], first[:, 0:w - 1], pext[:, 16:16 + w - 1], ALU.subtract).then_inc(q_made, 1)
                link.on(copy(ptail[:, g, 0:PS], pext[:, 16 + T - PS:16 + T]))
                link.on(copy(ptail[:, g, PS:PS + NS], psmp[:, :, PS]))
                dve.wait_ge(q_made, g + 1)
                dve.wait_ge(q_round, g + 1)
                tt(ql[:], q32[:], qh[:].bitcast(F32), ALU.subtract).then_inc(q_ready, 1)
                for j in range(2):
                    t = 2 * g + j
                    at = base + (1 if j == 0 else 7)
                    c_pair, h_pair, b_pair = ((1, 2, 3), (0, 1, 2))[j]
                    dve.wait_ge(w_used, at + 2)
                    dve.wait_ge(c_copied, t + 1)
                    link.on(copy(usmp[:, :, 0:CS], conv_state[:, t]))
                    link.on(tt(uext[:, 2:2 + H], csb[:, 0:H], bank(h_pair, 0), ALU.mult))
                    then(tt(usmp[:, :, CS], csb[:, T:N], bank(h_pair, 1)[:, HB:H], ALU.mult))
                    tt(uext[:, 2 + H:2 + T], csb[:, H:T], bank(h_pair, 1)[:, 0:HB], ALU.mult).then_inc(u_made, 1)
                    dve.wait_ge(u_made, t + 1)
                    link.on(copy(utail[:, t, 0:CS], uext[:, T:T + 2]))
                    link.on(copy(utail[:, t, CS:CS + NS], usmp[:, :, CS]))
                    for i in range(3):
                        wi = par[:, 7 * K + i * K + t:7 * K + i * K + t + 1]
                        parts = ((ymix[:, 0:T], uext[:, i:i + T]), (ymix[:, T:N], usmp[:, :, i]))
                        for y, u in parts:
                            if i == 0:
                                link.on(ts(y, u, wi, None, ALU.mult))
                            else:
                                link.on(stt(y, u, wi, y, ALU.mult, ALU.add))
                        dve.wait_ge(p_link, link.n)
                    dve.wait_ge(w_used, at + 3)
                    tt(two(ymix[:]), two(ymix[:]), pair_of(b_pair), ALU.mult).then_inc(ya_made, 1)
                    dve.wait_ge(ya_made, t + 1)
                    dve.wait_ge(sga_made, t + 1)
                    tt(ymix[:], ymix[:], sga[:], ALU.mult).then_inc(a_gated, 1)
                    dve.wait_ge(yp_copied, t + 1)
                    dve.wait_ge(sgp_made, t + 1)
                    stt(vmix[:], yp[:, j, :], par[:, 6 * K + t:6 * K + t + 1], sgp[:],
                        ALU.mult, ALU.mult).then_inc(p_gated, 1)
                    dve.wait_ge(a_gated, t + 1)
                    dve.wait_ge(p_gated, t + 1)
                    tt(ymix[:], ymix[:], vmix[:], ALU.add).then_inc(m_made, 1)
                    dve.wait_ge(m_made, t + 1)
                    dve.wait_ge(m_round, t + 1)
                    tt(ml[:, t, :], ymix[:], mh[:, t, :].bitcast(F32), ALU.subtract).then_inc(m_ready, 1)
                scale_residual(1, (2 * g, 2 * g + 1))

            norm_steps(1, OUT, 1, 1.0)
            dve.wait_ge(tails_out, 64)
            up_steps(1)
            norm_steps(2, DOWN[1], 3, 0.5, last=True)
            for i, t in enumerate(range(ROWS_A, TT)):
                dve.wait_ge(y_turned, ROWS_A + i + 1)
                copy(yrow[:, t, 0:512], ps[:, ROW_BANK[t], :]).then_inc(y_copied[1], 1)
            dve.wait_ge(y_turned, TURNED_LEFT)
            copy(ysrow[:, 0:512], ps[0:NS, ROW_BANK[TT], :]).then_inc(y_copied[1], 1)
            dve.wait_ge(y_turned, TURNED_LEFT + 2)
            copy(yrow[:, TT - 1, 512:1024], ps[:, ROW_BANK[TT - 1] + 1, :]).then_inc(y_copied[1], 1)

        @block.tensor
        def _(pe):
            mm = nc.tensor.matmul

            def run(out, blocks_, start=True, stop=True):
                count = sum(not callable(b) for b in blocks_)
                n = 0
                for b in blocks_:
                    if callable(b):
                        b()
                        continue
                    slot, k, vh, vl = b
                    n += 1
                    mm(out, wh[:, slot, k, :], vh, start=start and n == 1, stop=False)
                    mm(out, wh[:, slot, k, :], vl, start=False, stop=False)
                    ins = mm(out, wl[:, slot, k, :], vh, start=False, stop=stop and n == count)
                return ins

            def run_both(pair, slot, tiles, start=True, stop=True):
                count = sum(not callable(b) for b in tiles)
                n = 0
                for b in tiles:
                    if callable(b):
                        b()
                        continue
                    k, vh, vl = b
                    n += 1
                    for h in range(2):
                        mm(bank(pair, h), wh[:, slot, k, :], half(vh, h), start=start and n == 1, stop=False)
                        mm(bank(pair, h), wh[:, slot, k, :], half(vl, h), start=False, stop=False)
                    for h in range(2):
                        ins = mm(bank(pair, h), wl[:, slot, k, :], half(vh, h), start=False, stop=stop and n == count)
                return ins

            def product(c, place, pair):
                pe.wait_ge(lo_ready, c + 1)
                run_both(pair, place % SLOTS, [(k, xh[:, k, :], xl[:, k, :]) for k in range(K)]).then_inc(w_used, 1)

            def first_opening():
                def one_pass(j, w, x, each=None, stop=False):
                    for k in range(K):
                        if each:
                            each(k)
                        for h in range(2):
                            ins = mm(bank(j, h), w[:, j, k, :], half(x[:, k, :], h),
                                     start=w is wh and x is xh and k == 0, stop=stop and k == K - 1)
                    return ins

                pe.wait_ge(x_round[1], 1)
                for j in range(2):
                    pe.wait_ge(x_read[0], j + 1)
                    pe.wait_ge(x_read[1], j + 1)
                    pe.wait_ge(hi_ready, j + 1)
                    one_pass(j, wh, xh, each=lambda k: pe.wait_ge(x_round[k % 2], k // 2 + 1 + k % 2))
                    pe.wait_ge(lo_ready, j + 1)
                    one_pass(j, wl, xh)
                parameter_transposes()
                for j in range(2):
                    one_pass(j, wh, xl, each=lambda k: pe.wait_ge(x_ready, k + 1), stop=True).then_inc(w_used, 1)
                product(2, 2, 2)
                pe.wait_ge(cols_read, 4)
                product(3, 3, 3)

            def opening(c, n, sums_at):
                def hi_products(j, k, h):
                    slot = (c + j) % SLOTS
                    mm(bank(j, h), wh[:, slot, k, :], half(xh[:, k, :], h), start=k == 0, stop=False)
                    mm(bank(j, h), wl[:, slot, k, :], half(xh[:, k, :], h), start=False, stop=False)

                def lo_products(j, h):
                    for k in range(K):
                        if j == 0 and k % 2 == 0:
                            pe.wait_ge(norm[n].ready, 4 * h + k // 2 + 1)
                        ins = mm(bank(j, h), wh[:, (c + j) % SLOTS, k, :], half(xl[:, k, :], h),
                                 start=False, stop=k == K - 1)
                    return ins

                def sums(h, place):
                    for at, what in zip(sums_at, (stat_sums, spread_sums)):
                        if h == 0 and at == place:
                            what(n, 1)

                for h in range(2):
                    for k in range(K):
                        if k % 2 == 0:
                            pe.wait_ge(norm[n].round, 4 * h + k // 2 + 1)
                        for j in range(3):
                            if h == 0 and k == 0:
                                pe.wait_ge(lo_ready, c + j + 1)
                            hi_products(j, k, h)
                        sums(h, k)
                    for j in range(4):
                        ins = lo_products(j, h)
                        if h == 1:
                            ins.then_inc(w_used, 1)
                        sums(h, K + j)
                        if j == 0:
                            if h == 0:
                                pe.wait_ge(lo_ready, c + 4)
                            for k in range(K):
                                hi_products(3, k, h)

            def shift_sums(n):
                s = norm[n]
                pe.wait_ge(s.turn, K + 2)
                for h in range(2):
                    mm(bank(2, h), ones_tile[:], half(xh[:, 0, :], h), start=True, stop=True).then_inc(s.shift, 1)

            def stat_sums(n, h):
                s = norm[n]
                additions = EARLY[n] - 1 + CLOSING[n] * (h + 1)
                for what, sums, done in ((0, tile_sum, s.c_sum), (4, square_sum, s.q_sum)):
                    pe.wait_ge(done, additions)
                    for b in range(4):
                        ins = mm(ps[0:HQ, h, what + b:what + b + 1], half(sums, h)[:, b * HQ:(b + 1) * HQ],
                                 ones_mean[:, 0:1], start=True, stop=True)
                ins.then_inc(s.stats, 1)

            def spread_sums(n, h):
                s = norm[n]
                for column, pair, ready in ((means, 1, 8 * h + 1), (root, 0, 8 * h + 8)):
                    pe.wait_ge(s.chain, ready)
                    for b in range(4):
                        ins = mm(bank(pair, h)[:, b * HQ:(b + 1) * HQ], column[:, b:b + 1].broadcast_to([HQ, P]),
                                 ident[0:HQ, 0:HQ], start=True, stop=True)
                    ins.then_inc(s.spread, 1)

            def closing(n, c, chunks_of, vectors, sums_at):
                s = norm[n]
                for h in range(2):
                    for i in range(CLOSING[n]):
                        if h == 0 and i < 2:
                            pe.wait_ge(s.centred, EARLY[n] - 1 + i)
                        for q in range(chunks_of):
                            ch = c + chunks_of * i + q
                            if h == 0:
                                pe.wait_ge(lo_ready, ch + 1)
                            blocks_ = vectors(ch, q, h)
                            for (at, after), sums in zip(sums_at, (stat_sums, spread_sums)):
                                if h == 1 and at == ch - c:
                                    blocks_.insert(after, lambda sums=sums: sums(n, 0))
                            ins = run(bank(i, h), blocks_, start=q == 0, stop=q == chunks_of - 1)
                            if h == 1:
                                ins.then_inc(w_used, 1)
                            elif q == chunks_of - 1:
                                ins.then_inc(s.half_done, 1)

            def down(n, d, j, first):
                for q, (k0, nk) in enumerate(DQ):
                    place = DOWN[n] + 3 * j + q
                    pe.wait_ge(lo_ready, d * 3 + (DOWN[n] + q + 1))
                    tiles = [(k, hid[n][0][:, k0 + k, :], hid[n][1][:, k0 + k, :]) for k in range(nk)]
                    if first and j == 0:
                        tiles = [x for k, tile in enumerate(tiles)
                                 for x in (lambda k=k: pe.wait_ge(ffn[n].hid_ready, k0 + k + 1), tile)]
                    if first and j == 1 and q == 0:
                        tiles.insert(5, lambda: shift_sums(2 * n))
                    run_both(j, place % SLOTS, tiles, start=q == 0, stop=q == len(DQ) - 1).then_inc(w_used, 1)

            def hid_blocks(n, ch, q, h):
                k0, nk = DQ[q]
                return [(ch % SLOTS, k, half(hid[n][0][:, k0 + k, :], h), half(hid[n][1][:, k0 + k, :], h))
                        for k in range(nk)]

            def ffn_steps(n):
                s = ffn[n]

                def up(f, place):
                    if isinstance(f, int) and f < 2:
                        return
                    pair = 2 * (place % 2)
                    pe.wait_ge(s.gated, f - 1)
                    product(2 * f + UP[n], 2 * place + UP[n], pair)
                    pe.wait_ge(s.hid_made, f - 1)
                    product(2 * f + (UP[n] + 1), 2 * place + UP[n] + 1, pair + 1)
                up_tiles(pe, up)
                pe.wait_ge(s.hid_made, KF - 1)
                down(n, 0, 0, True)
                pe.wait_ge(s.hid_made, KF)
                down(n, 1, 1, True)
                with pe.Fori(0, EARLY[2 * n] // 2 - 1) as i:
                    for j in range(2):
                        pe.wait_ge(norm[2 * n].centred, i * 2 + (j + 1))
                        down(n, i * 2 + (2 + j), j, False)
                closing(2 * n, DOWN[n] + 3 * EARLY[2 * n], 3, lambda ch, q, h: hid_blocks(n, ch, q, h),
                        ((0, 5), (1, 4)))

            def parameter_transposes():
                for parity in range(2):
                    pe.wait_ge(x_read[parity], K // 2)
                pe.wait_ge(small_in, 16 * 10)
                cw, pw = NS * CS, NS * PS
                for k in range(K):
                    nc.tensor.transpose(ps[:, 7, 128 + k * cw:128 + (k + 1) * cw], csrow[:, k * P:(k + 1) * P],
                                        ident[0:cw, 0:cw])
                nc.tensor.transpose(ps[:, 7, 0:10 * K], prow[:], ident[0:10 * K, 0:10 * K])
                for g in range(G):
                    ins = nc.tensor.transpose(ps[:, 6, g * pw:(g + 1) * pw], psrow[:, g * P:(g + 1) * P],
                                              ident[0:pw, 0:pw])
                ins.then_inc(cols_made, 1)

            pe.wait_ge(const_ready, 3)
            for _ in range(WARM_UP):
                nc.tensor.transpose(ps[:, 6, 0:P], ident[:], ident[:])
            pe.wait_ge(sample_in, 16)
            for k in range(K):
                ins = nc.tensor.transpose(ps[:, 7, k * NS:(k + 1) * NS], srow[:, k * P:(k + 1) * P],
                                          ident[0:NS, 0:NS])
            ins.then_inc(cols_made, 1)
            for t in range(TT):
                pe.wait_ge(rows_in[t], 16)
                for k in range(K):
                    if t == 0 and k == 7:
                        pe.wait_ge(cols_read, 1)
                    ins = nc.tensor.transpose(ps[:, k, t * P:(t + 1) * P], xrow[:, t, k * P:(k + 1) * P], ident[:])
                    if t == TT - 1:
                        ins.then_inc(cols_made, 1)

            first_opening()
            ffn_steps(0)

            def mix_group(g, opened):
                def wproduct(at, pair):
                    product(g * 12 + (MIX + at), MIX + at, pair)

                if not opened:
                    pe.wait_ge(yp_copied, g * 2 - 1)
                    wproduct(0, 0)
                    pe.wait_ge(sgp_made, g * 2)
                    wproduct(1, 1)
                    pe.wait_ge(ya_made, g * 2)
                    wproduct(2, 2)
                    pe.wait_ge(sga_made, g * 2)
                    wproduct(3, 3)
                pe.wait_ge(lo_ready, g * 12 + (MIX + 5))
                pe.wait_ge(q_ready, g + 1)
                pe.wait_ge(c_copied, g * 2 + 1)
                slot = (MIX + 4) % SLOTS
                for j in range(2):
                    for h in range(2):
                        ins = run(bank(j, h), [(slot, j, half(qh[:], h), half(ql[:], h))])
                ins.then_inc(w_used, 1)
                pe.wait_ge(u_made, g * 2 + 1)
                wproduct(5, 2)
                pe.wait_ge(ya_made, g * 2 + 1)
                wproduct(6, 3)
                pe.wait_ge(yp_copied, g * 2 + 1)
                wproduct(7, 0)
                pe.wait_ge(yp_copied, g * 2 + 2)
                wproduct(8, 1)
                pe.wait_ge(sga_made, g * 2 + 1)
                wproduct(9, 2)
                pe.wait_ge(sgp_made, g * 2 + 1)
                wproduct(10, 3)
                pe.wait_ge(u_made, g * 2 + 2)
                wproduct(11, 1)

            opening(MIX, 0, (3, 6))
            mix_group(0, True)
            with pe.Fori(1, G) as g:
                mix_group(g, False)

            def m_tiles(ks):
                return [(k, mh[:, k, :], ml[:, k, :]) for k in ks]

            pe.wait_ge(c_copied, K)
            pe.wait_ge(lo_ready, OUT + 1)
            pe.wait_ge(m_ready, K - 1)
            run_both(0, OUT % SLOTS, m_tiles(range(K - 1)), stop=False)
            pe.wait_ge(m_ready, K)
            run_both(0, OUT % SLOTS, m_tiles([K - 1]), start=False).then_inc(w_used, 1)
            for d in range(1, EARLY[1]):
                if d == 1:
                    pe.wait_ge(sgp_made, K)
                else:
                    pe.wait_ge(norm[1].centred, d - 1)
                pe.wait_ge(lo_ready, OUT + d + 1)
                tiles = m_tiles(range(K))
                if d == 1:
                    tiles.insert(4, lambda: shift_sums(1))
                run_both(d % 2, (OUT + d) % SLOTS, tiles).then_inc(w_used, 1)
                if d == 2:
                    pe.wait_ge(norm[1].shifted, K - 1)
                    for g in range(G):
                        nc.tensor.transpose(ps[0:PS + NS, 4, g * P:(g + 1) * P], ptail[:, g, :], ident[:])
                    for t in range(K):
                        ins = nc.tensor.transpose(ps[0:CS + NS, 6 + t // 4, (t % 4) * P:(t % 4 + 1) * P],
                                                  utail[:, t, :], ident[:])
                    ins.then_inc(tails_turned, 1)
            pe.wait_ge(tails_copied, 3)
            closing(1, OUT + EARLY[1], 1,
                    lambda ch, q, h: [(ch % SLOTS, k, half(mh[:, k, :], h), half(ml[:, k, :], h)) for k in range(K)],
                    ((0, 5), (1, 4)))

            opening(UP[1], 1, (5, 8))
            ffn_steps(1)
            def to_rows(t, k):
                bank_at, cols = ROW_BANK[t] + k // 4, slice((k % 4) * P, (k % 4 + 1) * P)
                if t < TT:
                    return nc.tensor.transpose(ps[:, bank_at, cols], x32[:, k, t * P:(t + 1) * P], ident[:])
                return nc.tensor.transpose(ps[0:NS, bank_at, cols], x32[:, k, T:N], ident[:])

            assert ROWS_A == 2
            pe.wait_ge(norm[2].biased, 4)
            pe.wait_ge(norm[2].centred, K + CLOSING[2])
            for t in range(ROWS_A):
                for k in range(K):
                    ins = to_rows(t, k)
                ins.then_inc(y_turned, 1)
                if t == 0:
                    stat_sums(2, 1)
            spread_sums(2, 1)
            for _ in range(KEEP_WARM):
                nc.tensor.transpose(ps[:, ROW_BANK[TT - 1], 0:P], ident[:], ident[:])
            pe.wait_ge(y_copied[0], 2)
            for k in range(K):
                if k % 2 == 0:
                    pe.wait_ge(norm[2].biased, 4 + k // 2 + 1)
                for t in range(ROWS_A, TT + 1):
                    ins = to_rows(t, k)
                    if k % 4 == 3:
                        ins.then_inc(y_turned, 1)


_INS = ["x_prompt", "x_sample", "state_conv", "state_pool", "ln1_g", "ln1_b", "ffn1_wg", "ffn1_wu", "ffn1_wd",
        "w_in", "conv_w", "pool_w", "pool_scale", "w_out", "ln2_g", "ln2_b", "ffn2_wg", "ffn2_wu", "ffn2_wd",
        "ln3_g", "ln3_b"]


def kernel(**inputs):
    import numpy as _np
    import concourse.bacc as _bacc
    from concourse import mybir as _mybir
    from concourse.bass_utils import run_bass_kernel_spmd as _run

    nc = _bacc.Bacc("TRN2", target_bir_lowering=False, num_devices=1)
    arrays, args = {}, []
    for name in _INS:
        a = _np.ascontiguousarray(inputs[name])
        arrays[f"in_{name}_dram"] = a
        args.append(nc.dram_tensor(f"in_{name}_dram", a.shape, _mybir.dt.from_np(a.dtype), kind="ExternalInput").ap())
    depth, batch, cs, d = inputs["state_conv"].shape
    _, _, ps, dp = inputs["state_pool"].shape
    pb = inputs["x_prompt"].shape[0]
    outs = [inputs["x_prompt"].shape, inputs["x_sample"].shape, (depth, pb, cs, d), (depth, pb, ps, dp),
            (depth, batch, cs, d), (depth, batch, ps, dp)]
    for i, shape in enumerate(outs):
        args.append(nc.dram_tensor(f"out_{i}_dram", shape, F32, kind="ExternalOutput").ap())
    build(nc, *args)
    r = _run(nc, [arrays], core_ids=[0])
    return tuple(r.results[0][f"out_{i}_dram"] for i in range(len(outs)))
```
